# Optimizing a Trainium2 kernel written in Bass

```python
import jax, jax.numpy as jnp
from jax import lax
import numpy as np
import math
import jax
import jax.numpy as jnp

D_MODEL = 1024
BATCH = 1
SEQ = 256
DEPTH = 2

HEAD_DIM = 64
N_FOX = 6
N_DSA = 5
N_SB = 5
N_IDX_HEADS = 8
IDX_DIM = 64
TOPK_MAX = 256
N_MEM = 256
N_CA_HEADS = 4
CA_HEAD_DIM = 128
D_FF = 2816
ROPE_THETA = 10000.0
Q_BLOCK = 128
NORM_EPS = 1e-6
N_BRANCH = 3
HALF_STEP = 0.5
FGATE_BIAS_OFFSET = 3.0

FOX_W = N_FOX * HEAD_DIM
DSA_W = N_DSA * HEAD_DIM
SB_W = N_SB * HEAD_DIM
CA_W = N_CA_HEADS * CA_HEAD_DIM
IN_SPLITS = (3 * FOX_W, N_FOX, 3 * DSA_W, N_IDX_HEADS * IDX_DIM, IDX_DIM, N_IDX_HEADS, 3 * SB_W, N_BRANCH * D_MODEL)
D_IN = 3 * FOX_W + N_FOX + 3 * DSA_W + N_IDX_HEADS * IDX_DIM + IDX_DIM + N_IDX_HEADS + 3 * SB_W + N_BRANCH * D_MODEL


def rms_norm(x, g):
    xf = x.astype(jnp.float32)
    y = xf * lax.rsqrt(jnp.mean(xf * xf, axis=-1, keepdims=True) + NORM_EPS) * g.astype(jnp.float32)
    return y.astype(x.dtype)

def apply_rope(x, positions):
    d = x.shape[-1]
    half = d // 2
    inv_freq = jnp.power(ROPE_THETA, -jnp.arange(half, dtype=jnp.float32) * (2.0 / d))
    ang = positions.astype(jnp.float32)[..., None] * inv_freq
    cos = jnp.cos(ang)[:, :, None, :]
    sin = jnp.sin(ang)[:, :, None, :]
    xf = x.astype(jnp.float32)
    x1, x2 = xf[..., :half], xf[..., half:]
    return jnp.concatenate([x1 * cos - x2 * sin, x2 * cos + x1 * sin], axis=-1).astype(x.dtype)

def swiglu(h, w_gu, w_down):
    g, u = jnp.split(h @ w_gu, 2, axis=-1)
    return (jax.nn.silu(g) * u) @ w_down

def sweep_query_blocks(block_fn, seq_len):
    n_blocks = seq_len // Q_BLOCK
    out = lax.map(block_fn, jnp.arange(n_blocks, dtype=jnp.int32) * Q_BLOCK)
    out = jnp.moveaxis(out, 0, 1)
    return out.reshape((out.shape[0], seq_len) + out.shape[3:])

def fox_attention(q, k, v, log_f):
    seq_len, d = q.shape[1], q.shape[-1]
    scale = d ** -0.5
    c = jnp.cumsum(log_f, axis=1).transpose(0, 2, 1)
    key_pos = jnp.arange(seq_len)

    def block(start):
        qb = lax.dynamic_slice_in_dim(q, start, Q_BLOCK, axis=1)
        cb = lax.dynamic_slice_in_dim(c, start, Q_BLOCK, axis=2)
        logits = jnp.einsum('bqhd,bkhd->bhqk', qb, k).astype(jnp.float32) * scale
        logits = logits + cb[..., :, None] - c[:, :, None, :]
        qpos = start + jnp.arange(Q_BLOCK)
        causal = key_pos[None, :] <= qpos[:, None]
        p = jax.nn.softmax(jnp.where(causal, logits, -jnp.inf), axis=-1)
        return jnp.einsum('bhqk,bkhd->bqhd', p.astype(v.dtype), v)

    return sweep_query_blocks(block, seq_len)

def stick_breaking_attention(q, k, v):
    seq_len, d = q.shape[1], q.shape[-1]
    scale = d ** -0.5
    key_pos = jnp.arange(seq_len)

    def block(start):
        qb = lax.dynamic_slice_in_dim(q, start, Q_BLOCK, axis=1)
        z = jnp.einsum('bqhd,bkhd->bhqk', qb, k).astype(jnp.float32) * scale
        qpos = start + jnp.arange(Q_BLOCK)
        strict = key_pos[None, :] < qpos[:, None]
        log_beta = jax.nn.log_sigmoid(z)
        log_1m_beta = jnp.where(strict, jax.nn.log_sigmoid(-z), 0.0)
        after = lax.cumsum(log_1m_beta, axis=3, reverse=True) - log_1m_beta
        a = jnp.where(strict, jnp.exp(log_beta + after), 0.0)
        return jnp.einsum('bhqk,bkhd->bqhd', a.astype(v.dtype), v)

    return sweep_query_blocks(block, seq_len)

def dsa_sparse_attention(q, k, v, q_idx, k_idx, w_idx, topk):
    seq_len, d = q.shape[1], q.shape[-1]
    scale = d ** -0.5
    key_pos = jnp.arange(seq_len)

    def block(start):
        qb = lax.dynamic_slice_in_dim(q, start, Q_BLOCK, axis=1)
        qib = lax.dynamic_slice_in_dim(q_idx, start, Q_BLOCK, axis=1)
        wb = lax.dynamic_slice_in_dim(w_idx, start, Q_BLOCK, axis=1)
        head_scores = jax.nn.relu(jnp.einsum('bqhd,bkd->bqhk', qib, k_idx).astype(jnp.float32))
        score = jnp.einsum('bqhk,bqh->bqk', head_scores, wb)
        qpos = start + jnp.arange(Q_BLOCK)
        causal = key_pos[None, :] <= qpos[:, None]
        score = jnp.where(causal[None], score, -jnp.inf)
        _, idx = lax.top_k(score, topk)
        valid = idx <= qpos[None, :, None]
        gather = jax.vmap(lambda arr, ii: arr[ii])
        k_sel = gather(k, idx)
        v_sel = gather(v, idx)
        logits = jnp.einsum('bqhd,bqkhd->bhqk', qb, k_sel).astype(jnp.float32) * scale
        logits = jnp.where(valid[:, None], logits, -jnp.inf)
        p = jax.nn.softmax(logits, axis=-1)
        return jnp.einsum('bhqk,bqkhd->bqhd', p.astype(v_sel.dtype), v_sel)

    return sweep_query_blocks(block, seq_len)

def hybrid_mixer(h, positions, w_in, b_fgate, w_fox_out, w_dsa_out, w_sb_out, w_out):
    b, s, _ = h.shape
    proj = h @ w_in
    offsets = np.cumsum(np.array(IN_SPLITS))[:-1].tolist()
    fox_qkv, fox_f, dsa_qkv, idx_q, idx_k, idx_w, sb_qkv, gates = jnp.split(proj, offsets, axis=-1)

    fq, fk, fv = [t[:, :, 0] for t in jnp.split(fox_qkv.reshape(b, s, 3, N_FOX, HEAD_DIM), 3, axis=2)]
    log_f = jax.nn.log_sigmoid(fox_f.astype(jnp.float32) + b_fgate.astype(jnp.float32))
    o_fox = fox_attention(fq, fk, fv, log_f).reshape(b, s, FOX_W)

    dq, dk, dv = [t[:, :, 0] for t in jnp.split(dsa_qkv.reshape(b, s, 3, N_DSA, HEAD_DIM), 3, axis=2)]
    dq = apply_rope(dq, positions)
    dk = apply_rope(dk, positions)
    q_idx = apply_rope(idx_q.reshape(b, s, N_IDX_HEADS, IDX_DIM), positions)
    k_idx = apply_rope(idx_k.reshape(b, s, 1, IDX_DIM), positions)[:, :, 0]
    w_idx = idx_w.astype(jnp.float32) * (N_IDX_HEADS ** -0.5) * (IDX_DIM ** -0.5)
    topk = min(TOPK_MAX, s // 4)
    o_dsa = dsa_sparse_attention(dq, dk, dv, q_idx, k_idx, w_idx, topk).reshape(b, s, DSA_W)

    sq, sk, sv = [t[:, :, 0] for t in jnp.split(sb_qkv.reshape(b, s, 3, N_SB, HEAD_DIM), 3, axis=2)]
    o_sb = stick_breaking_attention(sq, sk, sv).reshape(b, s, SB_W)

    g = jax.nn.sigmoid(gates.reshape(b, s, N_BRANCH, D_MODEL))
    merged = g[:, :, 0] * (o_fox @ w_fox_out) + g[:, :, 1] * (o_dsa @ w_dsa_out) + g[:, :, 2] * (o_sb @ w_sb_out)
    return merged @ w_out

def memory_cross_attention(h, mem_n, w_q, w_kv, w_o):
    b, s, _ = h.shape
    q = (h @ w_q).reshape(b, s, N_CA_HEADS, CA_HEAD_DIM)
    k, v = jnp.split((mem_n @ w_kv).reshape(b, mem_n.shape[1], 2, N_CA_HEADS, CA_HEAD_DIM), 2, axis=2)
    k, v = k[:, :, 0], v[:, :, 0]
    logits = jnp.einsum('bshd,bmhd->bhsm', q, k).astype(jnp.float32) * (CA_HEAD_DIM ** -0.5)
    p = jax.nn.softmax(logits, axis=-1)
    o = jnp.einsum('bhsm,bmhd->bshd', p.astype(v.dtype), v).reshape(b, s, CA_W)
    return o @ w_o

def first_inputs(seed: int = 0) -> dict:
    key = jax.random.key(seed)
    ks = jax.random.split(key, 24)
    f32 = jnp.float32

    def dense(k, shape):
        return jax.random.normal(k, shape, f32) * (shape[-2] ** -0.5)

    def gain(k, shape):
        return 1.0 + 0.02 * jax.random.normal(k, shape, f32)

    return {
        'x': jax.random.normal(ks[0], (BATCH, SEQ, D_MODEL), f32),
        'mem': jax.random.normal(ks[1], (BATCH, N_MEM, D_MODEL), f32),
        'positions': jnp.broadcast_to(jnp.arange(SEQ, dtype=jnp.int32), (BATCH, SEQ)),
        'ffn1_norm': gain(ks[2], (DEPTH, D_MODEL)),
        'ffn1_w_gu': dense(ks[3], (DEPTH, D_MODEL, 2 * D_FF)),
        'ffn1_w_down': dense(ks[4], (DEPTH, D_FF, D_MODEL)),
        'mix_norm': gain(ks[5], (DEPTH, D_MODEL)),
        'w_in': dense(ks[6], (DEPTH, D_MODEL, D_IN)),
        'b_fgate': FGATE_BIAS_OFFSET + 0.1 * jax.random.normal(ks[7], (DEPTH, N_FOX), f32),
        'w_fox_out': dense(ks[8], (DEPTH, FOX_W, D_MODEL)),
        'w_dsa_out': dense(ks[9], (DEPTH, DSA_W, D_MODEL)),
        'w_sb_out': dense(ks[10], (DEPTH, SB_W, D_MODEL)),
        'w_out': dense(ks[11], (DEPTH, D_MODEL, D_MODEL)),
        'ca_norm': gain(ks[12], (DEPTH, D_MODEL)),
        'mem_norm': gain(ks[13], (DEPTH, D_MODEL)),
        'ca_w_q': dense(ks[14], (DEPTH, D_MODEL, CA_W)),
        'ca_w_kv': dense(ks[15], (DEPTH, D_MODEL, 2 * CA_W)),
        'ca_w_o': dense(ks[16], (DEPTH, CA_W, D_MODEL)),
        'ffn2_norm': gain(ks[17], (DEPTH, D_MODEL)),
        'ffn2_w_gu': dense(ks[18], (DEPTH, D_MODEL, 2 * D_FF)),
        'ffn2_w_down': dense(ks[19], (DEPTH, D_FF, D_MODEL)),
        'final_norm': gain(ks[20], (D_MODEL,)),
    }

def first_block(x, mem, positions, ffn1_norm, ffn1_w_gu, ffn1_w_down, mix_norm, w_in, b_fgate, w_fox_out, w_dsa_out, w_sb_out, w_out, ca_norm, mem_norm, ca_w_q, ca_w_kv, ca_w_o, ffn2_norm, ffn2_w_gu, ffn2_w_down, final_norm):
    for l in range(DEPTH):
        x = x + HALF_STEP * swiglu(rms_norm(x, ffn1_norm[l]), ffn1_w_gu[l], ffn1_w_down[l])
        x = x + hybrid_mixer(rms_norm(x, mix_norm[l]), positions, w_in[l], b_fgate[l], w_fox_out[l], w_dsa_out[l], w_sb_out[l], w_out[l])
        x = x + memory_cross_attention(rms_norm(x, ca_norm[l]), rms_norm(mem, mem_norm[l]), ca_w_q[l], ca_w_kv[l], ca_w_o[l])
        x = x + HALF_STEP * swiglu(rms_norm(x, ffn2_norm[l]), ffn2_w_gu[l], ffn2_w_down[l])
    return rms_norm(x, final_norm)


MIX_WIDTH = D_MODEL
SSD_HEADS = 8
SSD_HEAD_DIM = 64
SSD_INNER = SSD_HEADS * SSD_HEAD_DIM
SSD_GROUPS = 2
SSD_STATE = 128
SSD_CONV = 4
SSD_CHUNK = 256
SSD_XBC = SSD_INNER + 2 * SSD_GROUPS * SSD_STATE
SC_HEADS = 4
SC_HEAD_DIM = 64
SC_WIDTH = SC_HEADS * SC_HEAD_DIM
SC_CONV = 3
NSA_HEADS = 4
NSA_HEAD_DIM = 64
NSA_WIDTH = NSA_HEADS * NSA_HEAD_DIM
NSA_KV = NSA_HEAD_DIM
CMP_BLOCK = 32
CMP_STRIDE = 16
CMP_HIDDEN = 128
SEL_BLOCK = 64
SEL_TOPK = 16
SEL_LOCAL = 2
WINDOW = 512
D_FF_2 = 2752
FFN_CONV = 3
EPS = 1e-6
NEG = -1e30
FORCE = 1e9
IN_SIZES = (SSD_INNER, SSD_XBC, SSD_HEADS, SC_WIDTH, SC_WIDTH, SC_WIDTH, NSA_WIDTH,
            NSA_KV, NSA_KV, NSA_KV, NSA_KV, NSA_KV, NSA_KV, 3 * NSA_HEADS)
N_IN = sum(IN_SIZES)


def rmsnorm(x, w):
    xf = x.astype(jnp.float32)
    y = xf * lax.rsqrt(jnp.mean(xf * xf, axis=-1, keepdims=True) + EPS)
    return (y * w.astype(jnp.float32)).astype(x.dtype)

def causal_dwconv(u, w, b=None):
    width = w.shape[0]
    s_len = u.shape[1]
    up = jnp.pad(u, ((0, 0), (width - 1, 0), (0, 0)))
    out = up[:, 0:s_len] * w[0]
    for j in range(1, width):
        out = out + up[:, j:j + s_len] * w[j]
    if b is not None:
        out = out + b
    return out

def rope_tables(s_len):
    half = NSA_HEAD_DIM // 2
    inv = 1.0 / (ROPE_THETA ** (jnp.arange(half, dtype=jnp.float32) / half))
    ang = jnp.arange(s_len, dtype=jnp.float32)[:, None] * inv[None, :]
    return jnp.cos(ang), jnp.sin(ang)

def apply_rope_2(x, cos, sin):
    x1, x2 = jnp.split(x, 2, axis=-1)
    c = cos[None, :, None, :].astype(x.dtype)
    s = sin[None, :, None, :].astype(x.dtype)
    return jnp.concatenate([x1 * c - x2 * s, x2 * c + x1 * s], axis=-1)

def masked_softmax(s, mask):
    s = jnp.where(mask, s.astype(jnp.float32), NEG)
    m = jnp.max(s, axis=-1, keepdims=True)
    p = jnp.exp(s - m) * mask
    return p / jnp.maximum(jnp.sum(p, axis=-1, keepdims=True), 1e-20)

def ssd_mixer(z, xbc, dt_raw, conv_w, conv_b, dt_bias, a_log, d_skip, norm_w):
    f32 = jnp.float32
    bsz, s_len, _ = z.shape
    n_k = SSD_HEADS // SSD_GROUPS
    xbc = jax.nn.silu(causal_dwconv(xbc, conv_w, conv_b))
    xs, b_in, c_in = jnp.split(xbc, [SSD_INNER, SSD_INNER + SSD_GROUPS * SSD_STATE], axis=-1)
    dt = jax.nn.softplus((dt_raw + dt_bias).astype(f32))
    a_neg = -jnp.exp(a_log.astype(f32)).reshape(SSD_GROUPS, n_k)
    pad = (-s_len) % SSD_CHUNK
    s_pad = s_len + pad
    n_c = s_pad // SSD_CHUNK

    def chunked(t, *tail):
        t = jnp.pad(t.astype(f32), ((0, 0), (0, pad), (0, 0)))
        return t.reshape(bsz, n_c, SSD_CHUNK, *tail)

    x_c = chunked(xs, SSD_GROUPS, n_k, SSD_HEAD_DIM)
    dt_c = chunked(dt, SSD_GROUPS, n_k)
    b_c = chunked(b_in, SSD_GROUPS, SSD_STATE)
    c_c = chunked(c_in, SSD_GROUPS, SSD_STATE)
    xdt = x_c * dt_c[..., None]
    a = jnp.transpose(dt_c * a_neg, (0, 3, 4, 1, 2))
    a_cs = jnp.cumsum(a, axis=-1)
    causal = jnp.tril(jnp.ones((SSD_CHUNK, SSD_CHUNK), dtype=bool))
    seg = a_cs[..., :, None] - a_cs[..., None, :]
    decay = jnp.exp(jnp.where(causal, seg, -jnp.inf))
    cb = jnp.einsum('bclgn,bcsgn->bgcls', c_c, b_c)
    y_diag = jnp.einsum('bgkcls,bcsgkp->bclgkp', decay * cb[:, :, None], xdt)
    decay_to_end = jnp.exp(a_cs[..., -1:] - a_cs)
    chunk_states = jnp.einsum('bclgn,bgkcl,bclgkp->cbgkpn', b_c, decay_to_end, xdt)
    chunk_decay = jnp.moveaxis(jnp.exp(a_cs[..., -1]), -1, 0)

    def step(h, inp):
        s_new, d_c = inp
        return h * d_c[..., None, None] + s_new, h

    h0 = jnp.zeros((bsz, SSD_GROUPS, n_k, SSD_HEAD_DIM, SSD_STATE), f32)
    _, prev_states = lax.scan(step, h0, (chunk_states, chunk_decay))
    y_off = jnp.einsum('bclgn,cbgkpn,bgkcl->bclgkp', c_c, prev_states, jnp.exp(a_cs))
    y = y_diag + y_off + x_c * d_skip.astype(f32).reshape(SSD_GROUPS, n_k)[:, :, None]
    y = y.reshape(bsz, s_pad, SSD_INNER)[:, :s_len]
    y = y * jax.nn.silu(z.astype(f32))
    return rmsnorm(y, norm_w).astype(z.dtype)

def compress_block(t, pos, w1, w2):
    bsz, s_len, dk = t.shape
    n_cmp = (s_len - CMP_BLOCK) // CMP_STRIDE + 1
    idx = np.arange(n_cmp)[:, None] * CMP_STRIDE + np.arange(CMP_BLOCK)[None, :]
    blocks = (t[:, idx] + pos).reshape(bsz, n_cmp, CMP_BLOCK * dk)
    return jax.nn.gelu(blocks @ w1) @ w2

def nsa_mixer(q, k_cmp, v_cmp, k_sel, v_sel, k_win, v_win, gate_logits, cos, sin,
              kpos, kw1, kw2, vpos, vw1, vw2):
    bsz, s_len, _ = q.shape
    dk = NSA_HEAD_DIM
    q = apply_rope_2(q.reshape(bsz, s_len, NSA_HEADS, dk), cos, sin) * (dk ** -0.5)

    def rope_k(t):
        return apply_rope_2(t[:, :, None, :], cos, sin)[:, :, 0, :]

    kc = compress_block(rope_k(k_cmp), kpos, kw1, kw2)
    vc = compress_block(v_cmp, vpos, vw1, vw2)
    n_cmp = kc.shape[1]
    n_slc = s_len // SEL_BLOCK
    top = min(SEL_TOPK, n_slc)
    cmp_start = np.arange(n_cmp) * CMP_STRIDE
    slc_start = np.arange(n_slc) * SEL_BLOCK
    cmp_end = jnp.asarray(cmp_start + CMP_BLOCK - 1, jnp.int32)
    overlap = jnp.asarray(((cmp_start[:, None] < slc_start[None, :] + SEL_BLOCK)
                           & (cmp_start[:, None] + CMP_BLOCK > slc_start[None, :])).astype(np.float32))
    ks_blocks = rope_k(k_sel).reshape(bsz, n_slc, SEL_BLOCK, dk)
    vs_blocks = v_sel.reshape(bsz, n_slc, SEL_BLOCK, dk)
    win_pad = ((0, 0), (WINDOW, 0), (0, 0))
    kw = jnp.pad(rope_k(k_win), win_pad)
    vw = jnp.pad(v_win, win_pad)
    gates = jax.nn.sigmoid(gate_logits.astype(jnp.float32)).reshape(bsz, s_len, NSA_HEADS, 3)
    n_qb = s_len // Q_BLOCK

    def to_blocks(t):
        return jnp.moveaxis(t.reshape(bsz, n_qb, Q_BLOCK, *t.shape[2:]), 1, 0)

    blk = jnp.arange(n_slc)
    offs = jnp.arange(SEL_BLOCK)
    gather = jax.vmap(lambda blocks, idx: blocks[idx])

    def block_fn(args):
        qb, gb, qi = args
        t = qi * Q_BLOCK + jnp.arange(Q_BLOCK)
        p_c = masked_softmax(jnp.einsum('bqhd,bnd->bhqn', qb, kc), cmp_end[None, :] <= t[:, None])
        o_c = jnp.einsum('bhqn,bnd->bqhd', p_c, vc)
        imp = jnp.einsum('bhqn,nj->bqj', p_c, overlap)
        cur = (t // SEL_BLOCK)[:, None]
        valid = blk[None, :] <= cur
        forced = (blk[None, :] == 0) | (valid & (blk[None, :] > cur - SEL_LOCAL))
        imp = jnp.where(forced, FORCE, jnp.where(valid, imp, NEG))
        _, sel = lax.top_k(imp, top)
        ks = gather(ks_blocks, sel).reshape(bsz, Q_BLOCK, top * SEL_BLOCK, dk)
        vs = gather(vs_blocks, sel).reshape(bsz, Q_BLOCK, top * SEL_BLOCK, dk)
        tok = (sel[..., None] * SEL_BLOCK + offs).reshape(bsz, Q_BLOCK, top * SEL_BLOCK)
        m_s = (tok <= t[None, :, None])[:, None]
        p_s = masked_softmax(jnp.einsum('bqhd,bqnd->bhqn', qb, ks), m_s)
        o_s = jnp.einsum('bhqn,bqnd->bqhd', p_s, vs)
        start = qi * Q_BLOCK
        kwb = lax.dynamic_slice_in_dim(kw, start, Q_BLOCK + WINDOW, axis=1)
        vwb = lax.dynamic_slice_in_dim(vw, start, Q_BLOCK + WINDOW, axis=1)
        kp = start - WINDOW + jnp.arange(Q_BLOCK + WINDOW)
        m_w = (kp[None, :] >= 0) & (kp[None, :] <= t[:, None]) & (kp[None, :] > t[:, None] - WINDOW)
        p_w = masked_softmax(jnp.einsum('bqhd,bkd->bhqk', qb, kwb), m_w)
        o_w = jnp.einsum('bhqk,bkd->bqhd', p_w, vwb)
        return o_c * gb[..., 0:1] + o_s * gb[..., 1:2] + o_w * gb[..., 2:3]

    out = lax.map(block_fn, (to_blocks(q), to_blocks(gates), jnp.arange(n_qb)))
    return jnp.moveaxis(out, 0, 1).reshape(bsz, s_len, NSA_WIDTH).astype(q.dtype)

def second_inputs(seed: int = 0) -> dict:
    key = jax.random.key(seed)
    ks = jax.random.split(key, 24)
    f32 = jnp.float32
    nl = DEPTH
    cmp_in = CMP_BLOCK * NSA_HEAD_DIM

    def nrm(k, shape, scale):
        return jax.random.normal(k, shape, f32) * scale

    dt0 = jnp.exp(jax.random.uniform(ks[5], (nl, SSD_HEADS), f32, math.log(1e-3), math.log(1e-1)))
    return {
        'x': nrm(ks[0], (BATCH, SEQ, D_MODEL), 1.0),
        'attn_norm_w': 1.0 + nrm(ks[1], (nl, D_MODEL), 0.02),
        'w_in': nrm(ks[2], (nl, D_MODEL, N_IN), D_MODEL ** -0.5),
        'ssd_conv_w': nrm(ks[3], (nl, SSD_CONV, SSD_XBC), SSD_CONV ** -0.5),
        'ssd_conv_b': nrm(ks[4], (nl, SSD_XBC), 0.02),
        'ssd_dt_bias': dt0 + jnp.log(-jnp.expm1(-dt0)),
        'ssd_a_log': jnp.log(jax.random.uniform(ks[6], (nl, SSD_HEADS), f32, 1.0, 16.0)),
        'ssd_d': 1.0 + nrm(ks[7], (nl, SSD_HEADS), 0.02),
        'ssd_norm_w': 1.0 + nrm(ks[8], (nl, SSD_INNER), 0.02),
        'sc_conv_w': nrm(ks[9], (nl, SC_CONV, SC_WIDTH), SC_CONV ** -0.5),
        'cmp_k_pos': nrm(ks[10], (nl, CMP_BLOCK, NSA_HEAD_DIM), 0.02),
        'cmp_k_w1': nrm(ks[11], (nl, cmp_in, CMP_HIDDEN), cmp_in ** -0.5),
        'cmp_k_w2': nrm(ks[12], (nl, CMP_HIDDEN, NSA_HEAD_DIM), CMP_HIDDEN ** -0.5),
        'cmp_v_pos': nrm(ks[13], (nl, CMP_BLOCK, NSA_HEAD_DIM), 0.02),
        'cmp_v_w1': nrm(ks[14], (nl, cmp_in, CMP_HIDDEN), cmp_in ** -0.5),
        'cmp_v_w2': nrm(ks[15], (nl, CMP_HIDDEN, NSA_HEAD_DIM), CMP_HIDDEN ** -0.5),
        'w_out': nrm(ks[16], (nl, MIX_WIDTH, D_MODEL), MIX_WIDTH ** -0.5),
        'ffn_norm_w': 1.0 + nrm(ks[17], (nl, D_MODEL), 0.02),
        'ffn_w_up': nrm(ks[18], (nl, D_MODEL, 2 * D_FF_2), D_MODEL ** -0.5),
        'ffn_conv_w': nrm(ks[19], (nl, FFN_CONV, 2 * D_FF_2), FFN_CONV ** -0.5),
        'ffn_conv_b': nrm(ks[20], (nl, 2 * D_FF_2), 0.02),
        'ffn_w_down': nrm(ks[21], (nl, D_FF_2, D_MODEL), D_FF_2 ** -0.5),
        'final_norm_w': 1.0 + nrm(ks[22], (D_MODEL,), 0.02),
    }

def second_block(x, attn_norm_w, w_in, ssd_conv_w, ssd_conv_b, ssd_dt_bias, ssd_a_log, ssd_d,
              ssd_norm_w, sc_conv_w, cmp_k_pos, cmp_k_w1, cmp_k_w2, cmp_v_pos, cmp_v_w1, cmp_v_w2,
              w_out, ffn_norm_w, ffn_w_up, ffn_conv_w, ffn_conv_b, ffn_w_down, final_norm_w):
    s_len = x.shape[1]
    cos, sin = rope_tables(s_len)
    split_at = np.cumsum(np.array(IN_SIZES))[:-1].tolist()
    for l in range(DEPTH):
        h = rmsnorm(x, attn_norm_w[l])
        proj = h @ w_in[l]
        (z, xbc, dt_raw, sc_b, sc_c, sc_h, q, k_c, v_c, k_s, v_s, k_w, v_w,
         g_nsa) = jnp.split(proj, split_at, axis=-1)
        y_ssd = ssd_mixer(z, xbc, dt_raw, ssd_conv_w[l], ssd_conv_b[l], ssd_dt_bias[l],
                          ssd_a_log[l], ssd_d[l], ssd_norm_w[l])
        y_sc = sc_b * causal_dwconv(sc_c * sc_h, sc_conv_w[l])
        y_nsa = nsa_mixer(q, k_c, v_c, k_s, v_s, k_w, v_w, g_nsa, cos, sin,
                          cmp_k_pos[l], cmp_k_w1[l], cmp_k_w2[l],
                          cmp_v_pos[l], cmp_v_w1[l], cmp_v_w2[l])
        x = x + jnp.concatenate([y_ssd, y_sc, y_nsa], axis=-1) @ w_out[l]
        h = rmsnorm(x, ffn_norm_w[l])
        u = causal_dwconv(h @ ffn_w_up[l], ffn_conv_w[l], ffn_conv_b[l])
        gate, val = jnp.split(u, 2, axis=-1)
        x = x + (jax.nn.silu(gate) * val) @ ffn_w_down[l]
    return rmsnorm(x, final_norm_w)


def setup_inputs(seed=0):
    out = dict(first_inputs(seed))
    for name, value in second_inputs(seed + 1).items():
        if name != "x":
            out[name + "_2"] = value
    return out


def reference(
    x, mem, positions, ffn1_norm, ffn1_w_gu, ffn1_w_down, mix_norm, w_in, b_fgate, w_fox_out,
    w_dsa_out, w_sb_out, w_out, ca_norm, mem_norm, ca_w_q, ca_w_kv, ca_w_o, ffn2_norm,
    ffn2_w_gu, ffn2_w_down, final_norm, attn_norm_w_2, w_in_2, ssd_conv_w_2, ssd_conv_b_2,
    ssd_dt_bias_2, ssd_a_log_2, ssd_d_2, ssd_norm_w_2, sc_conv_w_2, cmp_k_pos_2, cmp_k_w1_2,
    cmp_k_w2_2, cmp_v_pos_2, cmp_v_w1_2, cmp_v_w2_2, w_out_2, ffn_norm_w_2, ffn_w_up_2,
    ffn_conv_w_2, ffn_conv_b_2, ffn_w_down_2, final_norm_w_2,
):
    x = first_block(
        x, mem, positions, ffn1_norm, ffn1_w_gu, ffn1_w_down, mix_norm, w_in, b_fgate,
        w_fox_out, w_dsa_out, w_sb_out, w_out, ca_norm, mem_norm, ca_w_q, ca_w_kv, ca_w_o,
        ffn2_norm, ffn2_w_gu, ffn2_w_down, final_norm,
    )
    return second_block(
        x, attn_norm_w_2, w_in_2, ssd_conv_w_2, ssd_conv_b_2, ssd_dt_bias_2, ssd_a_log_2,
        ssd_d_2, ssd_norm_w_2, sc_conv_w_2, cmp_k_pos_2, cmp_k_w1_2, cmp_k_w2_2, cmp_v_pos_2,
        cmp_v_w1_2, cmp_v_w2_2, w_out_2, ffn_norm_w_2, ffn_w_up_2, ffn_conv_w_2, ffn_conv_b_2,
        ffn_w_down_2, final_norm_w_2,
    )


_drawn_inputs = setup_inputs


def setup_inputs(seed=0):
    import zlib

    import numpy as np

    out = dict(_drawn_inputs(seed))
    spreads = {}
    factors = {'ca_norm': 6.855,
     'mem_norm': 6.093,
     'ssd_d_2': 5.052,
     'ssd_norm_w_2': 3.205,
     'cmp_k_pos_2': 64.0,
     'cmp_v_pos_2': 28.475,
     'ffn_norm_w_2': 3.147,
     'ffn_conv_b_2': 3.199,
     'final_norm_w_2': 8.691,
     'ffn2_norm': 3.374}
    for name, (base, spread) in spreads.items():
        noise = np.random.default_rng([zlib.crc32(name.encode()), seed]).standard_normal(out[name].shape)
        drawn = base * np.exp(spread * noise) if base else spread * noise
        out[name] = jnp.asarray(drawn.astype(out[name].dtype))
    for name, factor in factors.items():
        out[name] = (out[name] * factor).astype(out[name].dtype)
    return out
```

```python
import numpy as np
import concourse.bass as bass
from concourse import mybir
from contextlib import ExitStack, contextmanager

F32 = mybir.dt.float32
I32 = mybir.dt.int32
ALU = mybir.AluOpType
ACT = mybir.ActivationFunctionType
AX = mybir.AxisListType

P = 128
D = 1024
S = 256
T = S // P
C = D // P
DEPTH = 2
HD = 64
N_FOX, N_DSA, N_SB, N_IDX = 6, 5, 5, 8
FOX_W, DSA_W, SB_W = N_FOX * HD, N_DSA * HD, N_SB * HD
CA_H, CA_W = 4, 512
D_FF, D_FF2 = 2816, 2752
TOPK = min(256, S // 4)
EPS = 1e-6
NEG = -1e30
TAKEN = -3e38
RING = 4
SLOT = 2048
TRI = S + P

O_FQ, O_FK, O_FV = 0, FOX_W, 2 * FOX_W
O_FF = 3 * FOX_W
O_DQ = O_FF + N_FOX
O_DK, O_DV = O_DQ + DSA_W, O_DQ + 2 * DSA_W
O_IQ = O_DQ + 3 * DSA_W
O_IK = O_IQ + N_IDX * HD
O_IW = O_IK + HD
O_SQ = O_IW + N_IDX
O_SK, O_SV = O_SQ + SB_W, O_SQ + 2 * SB_W
O_G = O_SQ + 3 * SB_W
SSD_H, SSD_W = 8, 512
Z_Z, Z_X = 0, SSD_W
Z_DT = Z_X + 1024
Z_SC = Z_DT + SSD_H
Z_Q = Z_SC + 3 * 256
Z_KC = Z_Q + 256
Z_KS, Z_VS, Z_KW, Z_VW = Z_KC + 128, Z_KC + 192, Z_KC + 256, Z_KC + 320
Z_NG = Z_KC + 384
NSA_H = 4
CMP_BLOCK, CMP_STRIDE = 32, 16
N_CMP = (S - CMP_BLOCK) // CMP_STRIDE + 1


def constants():
    i = np.arange(P)
    inc = (i[:, None] <= i[None, :]).astype(np.float32)
    rot = np.zeros((P, P), np.float32)
    for m in range(P):
        if m % HD < HD // 2:
            rot[m + HD // 2, m] = -1.0
        else:
            rot[m - HD // 2, m] = 1.0
    half = HD // 2
    inv1 = np.power(np.float32(10000.0), -np.arange(half, dtype=np.float32) * np.float32(2.0 / HD)).astype(np.float32)
    inv2 = (np.float32(1.0) / np.power(np.float32(10000.0), np.arange(half, dtype=np.float32) / np.float32(half))).astype(np.float32)
    q = np.arange(S).reshape(T, P).T
    n = np.arange(16)
    cmp01 = ((n[None, None, :] * CMP_STRIDE + CMP_BLOCK - 1 <= q[:, :, None]) & (n < N_CMP)).astype(np.float32)
    tri_t = np.where(inc > 0, 0.0, NEG)
    one = np.ones((P, P), np.float32)
    parts = {
        "ident": np.eye(P),
        "upto": np.concatenate([inc, one], 1),
        "after": inc.T - np.eye(P),
        "rot": rot,
        "causal": np.concatenate([0 * one, np.where(inc.T > 0, 0.0, NEG)], 1),
        "causal_t": np.concatenate([tri_t, 0 * one, tri_t], 1),
        "strict_t": np.concatenate([inc - np.eye(P), one, inc - np.eye(P)], 1),
        "cmp01": cmp01.reshape(P, -1),
        "cmpneg": ((cmp01 - 1.0) * 1e30).reshape(P, -1),
        "inv1": np.tile(inv1, 4)[:, None],
        "inv2": np.tile(inv2, 4)[:, None],
        "pos2": np.tile(np.arange(S, dtype=np.float32)[None], (P, 1)),
    }
    at, offsets, arrays = 0, {}, []
    for name, a in parts.items():
        a = np.ascontiguousarray(a, dtype=np.float32)
        offsets[name] = (at, a.shape[1])
        arrays.append(a)
        at += a.shape[1]
    return offsets, np.concatenate(arrays, 1)


class Counts:

    def __init__(self, engine, plan, found):
        self.engine, self.plan, self.found, self.n, self.loops = engine, plan, found, {}, []

    def value(self, name):
        v = self.n.get(name, 0)
        for i, key in self.loops:
            k = self.plan.get((key, name), 0)
            if k:
                v = i * k + v
        return v

    def __call__(self, name, k=1):
        self.n[name] = self.n.get(name, 0) + k
        return self.value(name)

    @contextmanager
    def loop(self, eng, key, count):
        key = (self.engine, key)
        before = dict(self.n)
        with eng.Fori(0, count) as i:
            self.loops.append((i, key))
            yield i
            self.loops.pop()
        for name, v in self.n.items():
            k = v - before.get(name, 0)
            self.found[(key, name)] = k
            self.n[name] = before.get(name, 0) + count * k


class Banks:

    def __init__(self, n, where):
        self.n, self.where, self.k, self.pending = n, where, 0, ["dve_released"] * 4

    def oldest(self):
        name = self.pending.pop(0)
        return name, self.n(name)

    def take(self, kind, releaser="dve_released"):
        self.pending.append(releaser)
        self.where.setdefault(kind, []).append(self.k % 4)
        self.k += 1
        return (self.k - 1) % 4

    def skip(self):
        return -self.k % 4

    def released(self, name="dve_released"):
        return self.n.value(name) + sum(p == name for p in self.pending)


def build(nc, io, out, plan, found):
    const_at, _ = constants()
    n_const = sum(w for _, w in const_at.values())
    ctx = ExitStack()
    with ctx:
        ctx.enter_context(nc.allow_non_contiguous_dma(reason="a few broadcast vectors"))

        def sb(name, shape, dt=F32):
            return ctx.enter_context(nc.sbuf_tensor(name, shape, dt))

        ring = [sb(f"ring{r}", [P, SLOT]) for r in range(RING)]
        x = sb("x_sb", [P, T, D])
        mem = sb("mem_sb", [P, T, D])
        hT = sb("hT", [P, C, S])
        hs = sb("hs", [P, T, D])
        consts = sb("consts", [P, n_const])
        rope = sb("rope", [P, 2, 2, S])
        posi = sb("posi", [P, S], I32)
        work = sb("work", [P, 7680])
        arena = sb("arena", [P, 11100])
        gates = sb("gates", [P, 24, S])
        small = sb("small", [P, 400])
        vecs = sb("vecs", [P, 288])
        rows = sb("rows", [P, 4, P])
        bcast = sb("bcast", [P, 64])
        e4 = sb("e4", [P, 4, S])
        a4 = sb("a4", [P, 4, S])
        b4 = sb("b4", [P, 4, S])
        w2s = sb("w2s", [P, 192])
        topw = sb("topw", [P, T, S])
        dmask = sb("dmask", [P, T, S])
        bank = [ctx.enter_context(nc.psum_tensor(f"bank{i}", [P, 512], F32)) for i in range(8)]

        def K(name, a=0, b=None):
            o, w = const_at[name]
            return consts[:, o + a:o + (w if b is None else b)]

        ident = K("ident")
        ones = K("upto", P, 2 * P)
        incl = K("upto", 0, P)

        class Carve:
            def __init__(self, t, at=0):
                self.t, self.at = t, at

            def __call__(self, *dims):
                w = int(np.prod(dims))
                v = self.t[:, self.at:self.at + w]
                self.at += w
                assert self.at <= self.t.shape[1]
                if len(dims) == 2:
                    return v.rearrange("p (a b) -> p a b", b=dims[1])
                if len(dims) == 3:
                    return v.rearrange("p (a b c) -> p a b c", b=dims[1], c=dims[2])
                return v

        cw = Carve(work)
        guT = cw(22, S)
        cw = Carve(work)
        sc = cw(T, N_FOX, S)
        pT = cw(N_FOX, TRI)
        ixs = cw(N_IDX, S)
        cw = Carve(work)
        zS, lS, lbS, LS = (cw(N_SB, TRI) for _ in range(4))
        cw = Carve(work)
        csc, cpT = cw(T, CA_H, S), cw(CA_H, T * S)
        cw = Carve(work)
        nsc, npT = cw(T, 2 * NSA_H, S), cw(2 * NSA_H, TRI)
        cw = Carve(work)
        ssq = cw(C, S)
        ca = Carve(arena)
        fqT, fkT, dqT, dkT, iqT, ikT, sqT, skT = (ca(k, S) for k in (3, 3, 3, 3, 4, 1, 3, 3))
        V_F, V_FF, V_D = 0, FOX_W, FOX_W + N_FOX
        V_IW = V_D + DSA_W
        V_S = V_IW + N_IDX
        vtok = ca(T, V_S + SB_W)
        oT = ca(C, S)
        xr = ca(2, S)
        ca = Carve(arena)
        cqT, ckT, cv, coT = ca(CA_H, S), ca(CA_H, S), ca(T, CA_W), ca(CA_H, S)
        ca = Carve(arena)
        zT, xbc, scm = ca(4, S), ca(8, S), ca(6, S)
        nqT, kvT, ksT, kwT = ca(2, S), ca(1, S), ca(1, S), ca(1, S)
        vtok2 = ca(T, 148)
        cmpX = ca(CMP_BLOCK, N_CMP)
        yT = ca(C, S)
        pcT = ca(NSA_H, S)
        xr2 = ca(2, S)
        hid, kcT, vcs = ca(2, 16), ca(16), ca(64)
        g3 = gates[:, :, :].rearrange("p a b -> p (a b)")
        cg = Carve(g3)
        mT, cbT, xdt, zE = cg(SSD_H, TRI), cg(2, TRI), cg(T, SSD_W), cg(4, S)
        mT0 = g3[:, 0:C * S]
        hsT = hs[:, :, :].rearrange("p t d -> p (t d)").rearrange("p (c s) -> p c s", s=S)
        VEC2_DMAS, BC2_DMAS = 24, 7
        cs_ = Carve(small)
        ss, ms, rstd, nhalf = cs_(2), cs_(2), cs_(2), cs_(2)
        smax, ssum, mx8 = cs_(8), cs_(8), cs_(8)
        lf, lfn, lf2, lf3, cq = (cs_(T, 8) for _ in range(5))
        g12, g12e = cs_(T, 12), cs_(T, 12)
        csc8 = cs_(T, 8)
        cmpS = cs_(T, NSA_H, 16)
        anegs = cs_(8)
        hidE = cs_(2, N_CMP)

        sem = {name: ctx.enter_context(nc.semaphore(name)) for name in (
            [f"weights_in{r}" for r in range(RING)]
            + ["down_used",
               "up_done",
               "proj_done",
               "gate_done",
               "cmp_done",
               "attn_done",
               "pt_done",
               "dve_released",
               "act_released",
               "x_ready",
               "sq_done",
               "ms_done",
               "rstd_done",
               "h_scaled",
               "rows_in", "bcast_in",
               "gate_sigmoid",
               "conv_first",
               "gate_ready",
               "softplus_in", "softplus_out",
               "exp_in", "exp_out",
               "sigmoid_in", "sigmoid_out",
               "operand_ready",
               "io_in",
               "positions_in", "mem_in",
               "pool_ready",
               "sin_in", "sin_out",
               "hs_free", "final_in", "out_ready", "out_stored"])}

        where = {}
        pads = []
        seen_at = {}

        def seen(engine, kind, k=0):
            i = seen_at.get((engine, kind), 0)
            seen_at[engine, kind] = i + 1
            return bank[where[kind][i]]

        UP1 = ([("fq", i, O_FQ + P * i, P) for i in range(3)] + [("fk", i, O_FK + P * i, P) for i in range(3)]
               + [("iq", i, O_IQ + P * i, P) for i in range(4)] + [("ik", 0, O_IK, -HD)]
               + [("dq", i, O_DQ + P * i, min(P, DSA_W - P * i)) for i in range(3)]
               + [("dk", i, O_DK + P * i, min(P, DSA_W - P * i)) for i in range(3)]
               + [("sq", i, O_SQ + P * i, min(P, SB_W - P * i)) for i in range(3)]
               + [("sk", i, O_SK + P * i, min(P, SB_W - P * i)) for i in range(3)])
        DEST1 = dict(fq=fqT, fk=fkT, iq=iqT, ik=ikT, dq=dqT, dk=dkT, sq=sqT, sk=skT)
        ROPED = ("iq", "ik", "dq", "dk")
        TOK1 = [[(O_FV, 256, V_F)],
                [(O_FV + 256, P + N_FOX, V_F + 256), (O_IW, N_IDX, V_IW)],
                [(O_DV, 160, V_D)], [(O_DV + 160, 160, V_D + 160)],
                [(O_SV, 160, V_S)], [(O_SV + 160, 160, V_S + 160)]]
        UP2 = ([("z", i, Z_Z + P * i, P) for i in range(4)] + [("xbc", i, Z_X + P * i, P) for i in range(8)]
               + [("sc", i, Z_SC + P * i, P) for i in range(6)] + [("nq", i, Z_Q + P * i, P) for i in range(2)]
               + [("kv", 0, Z_KC, P), ("ks", 0, Z_KS, -HD), ("kw", 0, Z_KW, -HD)])
        TOK2 = [(Z_DT, 8, 0), (Z_VS, HD, 8), (Z_VW, HD, 8 + HD), (Z_NG, 12, 8 + 2 * HD)]

        def pairs(seq):
            return [seq[i:i + 2] for i in range(0, len(seq), 2)]

        def tile_parts(tiles):
            parts = []
            for j, (_, _, o, w) in enumerate(tiles):
                parts += [(j * P, o, -w), (j * P - w, o, -w)] if w < 0 else [(j * P, o, w)]
            return parts

        def tok_parts(cols):
            parts, a = [], 0
            for o, w, _ in cols:
                parts.append((a, o, w))
                a += w
            return parts

        block = ctx.enter_context(nc.Block())

        class Loader:
            def __init__(self, sp, n):
                self.sp, self.n, self.g, self.used = sp, n, 0, [("down_used", 1)] * RING

            def slot(self, used_by):
                name, k = self.used.pop(0)
                self.used.append(used_by)
                self.sp.wait_ge(sem[name], self.n(name, k))
                self.g += 1
                return (self.g - 1) % RING

            def cols(self, w, l, parts, used_by):
                r = self.slot(used_by)
                v = ring[r][:, :].rearrange("p (c n) -> p c n", n=S)
                for a, o, width in parts:
                    src = w[l, :, o:o + width] if isinstance(o, int) else w[l, :, bass.ds(o, width)]
                    self.sp.dma_start(v[:, :, a:a + width], src.rearrange("(c p) n -> p c n", p=P))\
                        .then_inc(sem[f"weights_in{r}"], 16)

            def rows(self, w, l, first, n_rows=2 * P):
                r = self.slot(("down_used", 1))
                v = ring[r][:, :].rearrange("p (c n) -> p c n", n=D)
                full = n_rows // P
                if isinstance(first, int):
                    src = w[l, first:first + full * P, :]
                else:
                    src = w[l, bass.ds(first, full * P), :]
                self.sp.dma_start(v[:, 0:full, :], src.rearrange("(c p) n -> p c n", p=P))\
                    .then_inc(sem[f"weights_in{r}"], 16)
                if n_rows % P:
                    self.sp.dma_start(v[0:n_rows % P, full, :], w[l, first + full * P:first + n_rows, :])\
                        .then_inc(sem[f"weights_in{r}"], 16)

            def ffn(self, key, w_gu, w_down, l, ff):
                n_f = -(-ff // P)
                def up(f, width=P):
                    self.cols(w_gu, l, [(0, f * P, width), (P, f * P + ff, width)], ("up_done", 2))
                for f in range(RING):
                    up(f)
                loops = n_f // RING - 1
                with self.n.loop(self.sp, key + "up", loops) as i:
                    for j in range(RING):
                        up(i * RING + (RING + j))
                for f in range(RING * (1 + loops), n_f):
                    up(f, min(P, ff - f * P))
                for f in range(-(-n_f // 2)):
                    self.rows(w_down, l, f * 2 * P, min(2 * P, ff - f * 2 * P))

        @block.sync
        def _(sp):
            n = Counts("sp", plan, found)
            ld = Loader(sp, n)
            sp.dma_start(x[:, :, :], io["x"][0].rearrange("(t p) d -> p t d", p=P)).then_inc(sem["io_in"], 16)
            sp.dma_start(consts[:, :], io["consts"]).then_inc(sem["io_in"], 16)
            with n.loop(sp, "block1", DEPTH) as l:
                ld.ffn("f1", io["ffn1_w_gu"], io["ffn1_w_down"], l, D_FF)
                for tiles in pairs(UP1):
                    ld.cols(io["w_in"], l, tile_parts(tiles), ("proj_done", len(tiles)))
                for cols in TOK1:
                    ld.cols(io["w_in"], l, tok_parts(cols), ("proj_done", T))
                for j in range(0, 24, 2):
                    ld.cols(io["w_in"], l, [(0, O_G + P * j, 2 * P)], ("gate_done", 2))
                for m in range(0, C, 2):
                    r = ld.slot(("proj_done", 6))
                    v = ring[r][:, :].rearrange("p (m k n) -> p m k n", m=2, k=C)
                    for j in range(2):
                        cols_ = slice((m + j) * P, (m + j + 1) * P)
                        for k0, w, k_n in ((0, "w_fox_out", 3), (3, "w_dsa_out", 2), (5, "w_sb_out", 2)):
                            sp.dma_start(v[:, j, k0:k0 + k_n, :],
                                         io[w][l, 0:k_n * P, cols_].rearrange("(k p) n -> p k n", p=P))\
                              .then_inc(sem[f"weights_in{r}"], 16)
                        for p0, w in ((0, "w_dsa_out"), (HD, "w_sb_out")):
                            sp.dma_start(v[p0:p0 + HD, j, 7, :], io[w][l, 2 * P:2 * P + HD, cols_])\
                              .then_inc(sem[f"weights_in{r}"], 16)
                for k in range(0, C, 2):
                    ld.rows(io["w_out"], l, k * P)
                for j in range(2):
                    ld.cols(io["ca_w_kv"], l, [(0, 2 * P * j, 2 * P)], ("proj_done", 2))
                for j in range(2):
                    ld.cols(io["ca_w_kv"], l, [(0, CA_W + 2 * P * j, 2 * P)], ("proj_done", 2))
                for j in range(2):
                    ld.cols(io["ca_w_q"], l, [(0, 2 * P * j, 2 * P)], ("proj_done", 2))
                for k in range(0, CA_H, 2):
                    ld.rows(io["ca_w_o"], l, k * P)
                ld.ffn("f2", io["ffn2_w_gu"], io["ffn2_w_down"], l, D_FF)
                assert ld.g % RING == 0, ld.g
            with n.loop(sp, "block2", DEPTH) as l:
                for tiles in pairs(UP2):
                    ld.cols(io["w_in_2"], l, tile_parts(tiles), ("proj_done", len(tiles)))
                ld.cols(io["w_in_2"], l, tok_parts(TOK2), ("proj_done", T))
                for half in range(2):
                    r = ld.slot(("cmp_done", 1))
                    v = ring[r][:, :].rearrange("p (j n) -> p j n", n=P)
                    for p0, w in ((0, "cmp_k_w1_2"), (HD, "cmp_v_w1_2")):
                        sp.dma_start(v[p0:p0 + HD, :, :],
                                     io[w][l, half * 1024:(half + 1) * 1024, :].rearrange("(j p) n -> p j n", p=HD))\
                          .then_inc(sem[f"weights_in{r}"], 16)
                for k in range(0, C, 2):
                    ld.rows(io["w_out_2"], l, k * P)
                ld.ffn("f3", io["ffn_w_up_2"], io["ffn_w_down_2"], l, D_FF2)
                assert ld.g % RING == 0, ld.g
            for t in range(T):
                sp.wait_ge(sem["out_ready"], t + 1)
                sp.dma_start(out[0, t * P:(t + 1) * P, :], hs[:, t, :]).then_inc(sem["out_stored"], 16)
            sp.wait_ge(sem["out_stored"], 16 * T)

        def sharing(heads):
            groups = [(h, h + 2) for h in range(heads) if h % 4 < 2]
            return [tuple(h for h in g if h < heads) for g in groups]

        def of(g):
            return slice(g[0], g[-1] + 1, 2)

        class Slots:

            def __init__(self, n):
                self.n, self.g = n, 0

            def next(self, loads):
                r = self.g % RING
                self.g += 1
                name = f"weights_in{r}"
                return ring[r][:, :], (sem[name], self.n(name, 16 * loads))

        def head(t, h):
            return t[HD * (h % 2):HD * (h % 2) + HD, h // 2, :]

        @block.tensor
        def _(pe):
            n = Counts("pe", plan, found)
            banks = Banks(n, where)
            slots = Slots(n)

            def free(kind, releaser="dve_released"):
                name, value = banks.oldest()
                pe.wait_ge(sem[name], value)
                return bank[banks.take(kind, releaser)]

            def up(b, view, a, width, src):
                for c in range(C):
                    mm = pe.matmul(b[0:width, 0:S], view[:, c, a:a + width], src[:, c, :],
                                   start=(c == 0), stop=(c == C - 1))
                return mm

            def tok(b, t, view, width, src):
                for c in range(C):
                    mm = pe.matmul(b[:, 0:width], src[:, c, t * P:(t + 1) * P], view[:, c, 0:width],
                                   start=(c == 0), stop=(c == C - 1))
                return mm

            def norm():
                pe.wait_ge(sem["h_scaled"], n("h_scaled", T))
                for g in range(C // 2):
                    b = free("attn_done")
                    for c in range(2):
                        for t in range(T):
                            mm = pe.transpose(b[:, c * S + t * P:c * S + (t + 1) * P],
                                              hs[:, t, (2 * g + c) * P:(2 * g + c + 1) * P], ident)
                    mm.then_inc(sem["attn_done"], 1)
                return sem["dve_released"], banks.released()

            def down(src, chunks, last_rows=P):
                for k in range(0, chunks, 2):
                    part = last_rows < P and k + 2 >= chunks
                    view, loaded = slots.next(2 if part else 1)
                    view = view.rearrange("p (c n) -> p c n", n=D)
                    pe.wait_ge(*loaded)
                    for j in range(2):
                        r = last_rows if k + j == chunks - 1 else P
                        for t in range(T):
                            for half in range(2):
                                mm = pe.matmul(bank[4 + 2 * t + half][:, :], src[0:r, k + j, t * P:(t + 1) * P],
                                               view[0:r, j, half * 512:(half + 1) * 512],
                                               start=(k + j == 0), stop=(k + j == chunks - 1))
                    mm.then_inc(sem["down_used"], 1)

            def ffn(key, ff):
                turned = norm()
                n_f = -(-ff // P)

                def one(width=P):
                    view, loaded = slots.next(2)
                    view = view.rearrange("p (c n) -> p c n", n=S)
                    pe.wait_ge(*loaded)
                    for half in range(2):
                        b = free("up_done")
                        up(b, view, half * P, width, hT).then_inc(sem["up_done"], 1)

                with n.loop(pe, key + "up", n_f // RING):
                    pe.wait_ge(*turned)
                    for _ in range(RING):
                        one()
                for f in range(n_f // RING * RING, n_f):
                    one(min(P, ff - f * P))
                if ff == D_FF:
                    pe.wait_ge(sem["dve_released"], banks.released())
                else:
                    pe.wait_ge(sem["operand_ready"], n("operand_ready"))
                down(guT, n_f, ff - (n_f - 1) * P)

            def vectors(loads, groups):
                pe.wait_ge(sem["rows_in"], n("rows_in", loads))
                b = free("attn_done")
                for g in range(groups):
                    mm = pe.transpose(b[:, g * P:(g + 1) * P], rows[:, g, :], ident)
                mm.then_inc(sem["attn_done"], 1)

            def proj(tiles_all, src, roped):
                late = []
                tile = 0
                for tiles in pairs(tiles_all):
                    view, loaded = slots.next(len(tile_parts(tiles)))
                    view = view.rearrange("p (c n) -> p c n", n=S)
                    pe.wait_ge(*loaded)
                    for j, (name, _, _, width) in enumerate(tiles):
                        w = P if width < 0 else width
                        b = free("proj_done")
                        up(b, view, j * P, w, src).then_inc(sem["proj_done"], 1)
                        copied = banks.released()
                        while late:
                            rotate(*late.pop(0))
                        if name in roped:
                            late.append((tile % 2, copied))
                            tile += 1
                while late:
                    rotate(*late.pop(0))

            def rotate(buf, copied):
                pe.wait_ge(sem["dve_released"], copied)
                b = free("attn_done")
                pe.matmul(b[:, 0:S], K("rot"), rope_src[0][:, buf, :], start=True, stop=True)\
                  .then_inc(sem["attn_done"], 1)

            rope_src = [xr]

            def tokens(loads, width, src):
                view, loaded = slots.next(loads)
                view = view.rearrange("p (c n) -> p c n", n=S)
                pe.wait_ge(*loaded)
                for t in range(T):
                    b = free("proj_done")
                    tok(b, t, view, width, src).then_inc(sem["proj_done"], 1)

            def gate_tiles(count):
                for _ in range(count // 2):
                    view, loaded = slots.next(1)
                    view = view.rearrange("p (c n) -> p c n", n=S)
                    pe.wait_ge(*loaded)
                    for j in range(2):
                        b = free("gate_done", "act_released")
                        up(b, view, j * P, P, hT).then_inc(sem["gate_done"], 1)

            def turn(p, h_n, kw=None):
                for h in range(h_n):
                    b = free("pt_done", "act_released")
                    for a, t, k in ((0, 0, 0), (P, 1, 0), (2 * P, 1, 1)):
                        mm = pe.transpose(b[:, a:a + P], p[:, t, h, k * P:(k + 1) * P], ident)
                    mm.then_inc(sem["pt_done"], 1)

            def weigh(b, p0, v, pt, start=True, stop=True):
                pe.matmul(b[p0:p0 + HD, 0:S], v[0], pt[:, 0:S], start=start, stop=False, skip_group_check=True)
                return pe.matmul(b[p0:p0 + HD, P:S], v[1], pt[:, S:TRI], start=False, stop=stop, skip_group_check=True)

            def end_layer():
                pads.append(banks.skip())
                if pads[-1]:
                    for _ in range(pads[-1]):
                        free("attn_done")
                    pe.drain().then_inc(sem["attn_done"], pads[-1])

            pe.sem_inc(sem["down_used"], RING)
            pe.sem_inc(sem["dve_released"], 4)
            pe.wait_ge(sem["io_in"], 32)

            with n.loop(pe, "block1", DEPTH):
                vectors(16 * 5, 1)
                ffn("f1", D_FF)
                pe.wait_ge(*norm())
                proj(UP1, hT, ROPED)
                for cols in TOK1:
                    tokens(len(cols), sum(w for _, w, _ in cols), hT)
                pe.wait_ge(sem["dve_released"], banks.released())
                for h in range(N_SB):
                    b = free("attn_done")
                    q, k = head(sqT, h), head(skT, h)
                    pe.matmul(b[:, 0:S], k[:, 0:P], q[:, :], start=True, stop=True)
                    pe.matmul(b[:, S:TRI], k[:, P:S], q[:, P:S], start=True, stop=True)\
                      .then_inc(sem["attn_done"], 1)
                gate_tiles(6)
                pe.wait_ge(sem["operand_ready"], n("operand_ready"))
                for h in range(N_SB):
                    b = free("attn_done")
                    pe.matmul(b[:, 0:S], K("after"), LS[:, h, 0:S], start=True, stop=False, skip_group_check=True)
                    pe.matmul(b[:, P:S], ones, LS[:, h, S:TRI], start=False, stop=True, skip_group_check=True)
                    pe.matmul(b[:, S:TRI], K("after"), LS[:, h, S:TRI], start=True, stop=True)\
                      .then_inc(sem["attn_done"], 1)
                pe.wait_ge(sem["operand_ready"], n("operand_ready"))
                b = free("attn_done")
                pe.matmul(b[:, 0:8], incl, lf[:, 0, :], start=True, stop=True)
                pe.matmul(b[:, 8:16], ones, lf[:, 0, :], start=True, stop=False)
                pe.matmul(b[:, 8:16], incl, lf[:, 1, :], start=False, stop=True).then_inc(sem["attn_done"], 1)
                gate_tiles(4)
                pe.wait_ge(sem["operand_ready"], n("operand_ready"))
                for i in range(3):
                    b = free("attn_done")
                    for h in range(2 * i, min(2 * i + 2, N_SB)):
                        p0 = HD if h == 4 else HD * (h % 2)
                        v = [vtok[:, t, V_S + HD * h:V_S + HD * (h + 1)] for t in range(T)]
                        mm = weigh(b, p0, v, zS[:, h, :])
                    mm.then_inc(sem["attn_done"], 1)
                for t in range(T):
                    w = P * (t + 1)
                    for g in sharing(N_FOX):
                        b = free("attn_done")
                        for j, h in enumerate(g):
                            o = b[:, j * S:j * S + w]
                            pe.matmul(o, head(fqT, h)[:, t * P:(t + 1) * P], head(fkT, h)[:, 0:w],
                                      start=True, stop=False, skip_group_check=True)
                            mm = pe.matmul(o, lfn[:, 0, h:h + 1].to_broadcast([P, P]), K("upto", 0, w),
                                           start=False, stop=(t == 0), skip_group_check=True)
                            if t == 1:
                                mm = pe.matmul(b[:, j * S + P:j * S + S], lfn[:, 1, h:h + 1].to_broadcast([P, P]),
                                               incl, start=False, stop=True, skip_group_check=True)
                        mm.then_inc(sem["attn_done"], 1)
                for t in range(T):
                    w = P * (t + 1)
                    for g in sharing(N_IDX):
                        b = free("attn_done")
                        for j, h in enumerate(g):
                            mm = pe.matmul(b[:, j * S:j * S + w], head(iqT, h)[:, t * P:(t + 1) * P],
                                           ikT[HD * (h % 2):HD * (h % 2) + HD, 0, 0:w], start=True, stop=True)
                        mm.then_inc(sem["attn_done"], 1)
                gate_tiles(8)
                pe.wait_ge(sem["operand_ready"], n("operand_ready"))
                turn(sc, N_FOX)
                pe.wait_ge(sem["act_released"], banks.released("act_released"))
                for i in range(N_FOX // 2):
                    b = free("attn_done")
                    for h in (2 * i, 2 * i + 1):
                        v = [vtok[:, t, V_F + HD * h:V_F + HD * (h + 1)] for t in range(T)]
                        mm = weigh(b, HD * (h % 2), v, pT[:, h, :])
                    mm.then_inc(sem["attn_done"], 1)
                for t in range(T):
                    w = P * (t + 1)
                    for g in sharing(N_DSA):
                        b = free("attn_done")
                        for j, h in enumerate(g):
                            mm = pe.matmul(b[:, j * S:j * S + w], head(dqT, h)[:, t * P:(t + 1) * P],
                                           head(dkT, h)[:, 0:w], start=True, stop=True)
                        mm.then_inc(sem["attn_done"], 1)
                gate_tiles(6)
                pe.wait_ge(sem["operand_ready"], n("operand_ready"))
                turn(sc, N_DSA)
                pe.wait_ge(sem["act_released"], banks.released("act_released"))
                for i in range(3):
                    b = free("attn_done")
                    for h in range(2 * i, min(2 * i + 2, N_DSA)):
                        v = [vtok[:, t, V_D + HD * h:V_D + HD * (h + 1)] for t in range(T)]
                        mm = weigh(b, HD * (h % 2), v, pT[:, h, :])
                    mm.then_inc(sem["attn_done"], 1)
                pe.wait_ge(sem["dve_released"], banks.released())
                for m in range(C):
                    if m % 2 == 0:
                        view, loaded = slots.next(10)
                        view = view.rearrange("p (m k n) -> p m k n", m=2, k=C)
                        pe.wait_ge(*loaded)
                    w = view[:, m % 2, :, :]
                    for own, tail in (((0, 1, 2), None), ((3, 4), 0), ((5, 6), HD)):
                        b = free("proj_done")
                        for k in own:
                            mm = pe.matmul(b[:, 0:S], w[:, k, :], oT[:, k, :], start=(k == own[0]),
                                           stop=(tail is None and k == own[-1]))
                        if tail is not None:
                            mm = pe.matmul(b[:, 0:S], w[tail:tail + HD, 7, :], oT[tail:tail + HD, 7, :],
                                           start=False, stop=True)
                        mm.then_inc(sem["proj_done"], 1)
                pe.wait_ge(sem["operand_ready"], n("operand_ready"))
                down(hsT, C)
                pe.wait_ge(*norm())
                for j in range(2):
                    view, loaded = slots.next(1)
                    view = view.rearrange("p (c n) -> p c n", n=S)
                    pe.wait_ge(*loaded)
                    for i in range(2):
                        b = free("proj_done")
                        up(b, view, i * P, P, hT).then_inc(sem["proj_done"], 1)
                for j in range(2):
                    tokens(1, 2 * P, hT)
                pe.wait_ge(*norm())
                for j in range(2):
                    view, loaded = slots.next(1)
                    view = view.rearrange("p (c n) -> p c n", n=S)
                    pe.wait_ge(*loaded)
                    for i in range(2):
                        b = free("proj_done")
                        up(b, view, i * P, P, hT).then_inc(sem["proj_done"], 1)
                pe.wait_ge(sem["dve_released"], banks.released())
                for t in range(T):
                    for i in range(2):
                        b = free("attn_done")
                        for j in range(2):
                            h = 2 * i + j
                            mm = pe.matmul(b[:, j * S:(j + 1) * S], cqT[:, h, t * P:(t + 1) * P], ckT[:, h, :],
                                           start=True, stop=True)
                        mm.then_inc(sem["attn_done"], 1)
                pe.wait_ge(sem["operand_ready"], n("operand_ready"))
                for h in range(CA_H):
                    b = free("pt_done", "act_released")
                    for k in range(T):
                        for t in range(T):
                            mm = pe.transpose(b[:, k * S + t * P:k * S + (t + 1) * P],
                                              csc[:, t, h, k * P:(k + 1) * P], ident)
                    mm.then_inc(sem["pt_done"], 1)
                pe.wait_ge(sem["act_released"], banks.released("act_released"))
                for h in range(CA_H):
                    b = free("attn_done")
                    for k in range(T):
                        mm = pe.matmul(b[:, 0:S], cv[:, k, h * P:(h + 1) * P], cpT[:, h, k * S:(k + 1) * S],
                                       start=(k == 0), stop=(k == T - 1))
                    mm.then_inc(sem["attn_done"], 1)
                pe.wait_ge(sem["dve_released"], banks.released())
                down(coT, CA_H)
                ffn("f2", D_FF)
                end_layer()

            rope_src[0] = xr2
            with n.loop(pe, "block2", DEPTH):
                vectors(16 * VEC2_DMAS, 4)
                pe.wait_ge(*norm())
                proj(UP2, hT, ("nq", "kv", "ks", "kw"))
                tokens(len(TOK2), 148, hT)
                pe.wait_ge(sem["operand_ready"], n("operand_ready"))
                bk, bv = free("cmp_tile"), free("cmp_tile")
                for half in range(2):
                    view, loaded = slots.next(2)
                    view = view.rearrange("p (j n) -> p j n", n=P)
                    pe.wait_ge(*loaded)
                    for b, p0 in ((bk, 0), (bv, HD)):
                        for j in range(16):
                            mm = pe.matmul(b[:, 0:N_CMP], view[p0:p0 + HD, j, :],
                                           cmpX[p0:p0 + HD, 16 * half + j, :],
                                           start=(half == 0 and j == 0), stop=(half == 1 and j == 15))
                    mm.then_inc(sem["cmp_done"], 1)
                pe.wait_ge(sem["operand_ready"], n("operand_ready"))
                for t in range(T):
                    b = free("attn_done")
                    for i in range(4):
                        mm = pe.transpose(b[:, i * P:(i + 1) * P], xbc[:, i, t * P:(t + 1) * P], ident)
                    mm.then_inc(sem["attn_done"], 1)
                for g in range(2):
                    b = free("attn_done")
                    pe.matmul(b[:, 0:S], xbc[:, 4 + g, 0:P], xbc[:, 6 + g, :], start=True, stop=True)
                    pe.matmul(b[:, S:TRI], xbc[:, 4 + g, P:S], xbc[:, 6 + g, P:S], start=True, stop=True)\
                      .then_inc(sem["attn_done"], 1)
                b = free("attn_done")
                pe.matmul(b[:, 0:8], incl, lf[:, 0, :], start=True, stop=True)
                pe.matmul(b[:, 8:16], ones, lf[:, 0, :], start=True, stop=False)
                pe.matmul(b[:, 8:16], incl, lf[:, 1, :], start=False, stop=True).then_inc(sem["attn_done"], 1)
                for h in range(SSD_H):
                    b = free("attn_done")
                    pe.matmul(b[:, 0:S], lf[:, 0, h:h + 1].to_broadcast([P, P]), K("upto"), start=True, stop=False,
                              skip_group_check=True)
                    pe.matmul(b[:, P:S], lf[:, 1, h:h + 1].to_broadcast([P, P]), incl, start=False, stop=True,
                              skip_group_check=True).then_inc(sem["attn_done"], 1)
                pe.wait_ge(sem["operand_ready"], n("operand_ready"))
                b = free("attn_done")
                pe.matmul(b[:, 0:N_CMP], w2s[:, 0:P], hid[:, 0, 0:N_CMP], start=True, stop=True)
                pe.matmul(b[0:N_CMP, 16:16 + HD], hid[:, 1, 0:N_CMP], w2s[:, P:P + HD], start=True, stop=True)\
                  .then_inc(sem["attn_done"], 1)
                pe.wait_ge(sem["dve_released"], banks.released())
                for g in sharing(NSA_H):
                    b = free("attn_done")
                    for t in range(T):
                        for j, h in enumerate(g):
                            a = (t * 2 + j) * 16
                            mm = pe.matmul(b[:, a:a + N_CMP], head(nqT, h)[:, t * P:(t + 1) * P],
                                           kcT[HD * (h % 2):HD * (h % 2) + HD, 0:N_CMP], start=True, stop=True)
                    mm.then_inc(sem["attn_done"], 1)
                for t in range(T):
                    w = P * (t + 1)
                    for kT in (ksT, kwT):
                        for g in sharing(NSA_H):
                            b = free("attn_done")
                            for j, h in enumerate(g):
                                mm = pe.matmul(b[:, j * S:j * S + w], head(nqT, h)[:, t * P:(t + 1) * P],
                                               kT[HD * (h % 2):HD * (h % 2) + HD, 0, 0:w], start=True, stop=True)
                            mm.then_inc(sem["attn_done"], 1)
                pe.wait_ge(sem["operand_ready"], n("operand_ready"))
                for i in range(SSD_H // 2):
                    b = free("attn_done")
                    for h in (2 * i, 2 * i + 1):
                        v = [xdt[:, t, HD * h:HD * (h + 1)] for t in range(T)]
                        mm = weigh(b, HD * (h % 2), v, mT[:, h, :])
                    mm.then_inc(sem["attn_done"], 1)
                pe.wait_ge(sem["operand_ready"], n("operand_ready"))
                b = free("attn_done")
                for i in range(4):
                    mm = pe.matmul(b[:, 0:S], ones, zE[:, i, :], start=(i == 0), stop=(i == 3))
                mm.then_inc(sem["attn_done"], 1)
                pe.wait_ge(sem["operand_ready"], n("operand_ready"))
                for t in range(T):
                    b = free("pt_done", "act_released")
                    for h in range(NSA_H):
                        mm = pe.transpose(b[0:N_CMP, h * P:(h + 1) * P], cmpS[:, t, h, 0:N_CMP], ident)
                    mm.then_inc(sem["pt_done"], 1)
                turn(nsc, 2 * NSA_H)
                pe.wait_ge(sem["act_released"], banks.released("act_released"))
                for i in range(NSA_H // 2):
                    b = free("attn_done")
                    for h in (2 * i, 2 * i + 1):
                        p0 = HD * (h % 2)
                        pe.matmul(b[p0:p0 + HD, 0:S], vcs[0:N_CMP, :], pcT[0:N_CMP, h, :], start=True, stop=False,
                                  skip_group_check=True)
                        vs = [vtok2[:, t, 8:8 + HD] for t in range(T)]
                        vw = [vtok2[:, t, 8 + HD:8 + 2 * HD] for t in range(T)]
                        weigh(b, p0, vs, npT[:, h, :], start=False, stop=False)
                        mm = weigh(b, p0, vw, npT[:, NSA_H + h, :], start=False, stop=True)
                    mm.then_inc(sem["attn_done"], 1)
                pe.wait_ge(sem["dve_released"], banks.released())
                pe.wait_ge(sem["operand_ready"], n("operand_ready"))
                down(yT, C)
                ffn("f3", D_FF2)
                end_layer()


        @block.scalar
        def _(act):
            n = Counts("act", plan, found)

            def load(dst, src, name):
                act.dma_start(dst, src).then_inc(sem[name], 16)

            def square_sums(src, wait_x=False):
                for t in range(T):
                    if wait_x:
                        act.wait_ge(sem["x_ready"], n("x_ready", 2))
                    act.activation(hs[:, t, :], src[:, t, :], ACT.Square, accum_out=ss[:, t:t + 1])\
                       .then_inc(sem["sq_done"], 1)

            def norm():
                square_sums(x, wait_x=True)

            def gate_tiles(first, count):
                for j in range(first, first + count):
                    act.wait_ge(sem["gate_done"], n("gate_done"))
                    act.activation(gates[:, j, :], seen("act", "gate_done")[:, 0:S], ACT.Sigmoid)\
                       .then_inc(sem["act_released"], 1)

            def exps(*parts):
                act.wait_ge(sem["exp_in"], n("exp_in"))
                for v in parts:
                    ins = act.activation(v, v, ACT.Exp)
                ins.then_inc(sem["exp_out"], 1)

            def sigmoids(*parts):
                act.wait_ge(sem["sigmoid_in"], n("sigmoid_in"))
                for v, s in parts:
                    ins = act.activation(v, v, ACT.Sigmoid, scale=s)
                ins.then_inc(sem["sigmoid_out"], 1)

            def softplus(v, src):
                act.wait_ge(sem["softplus_in"], n("softplus_in"))
                act.activation(v, src, ACT.Abs)
                act.drain()
                act.activation(v, v, ACT.Exp, scale=-1.0)
                act.drain()
                act.activation(v, v, ACT.Ln, bias=1.0).then_inc(sem["softplus_out"], 1)

            def turned(dst, h_n, w):
                for h in range(h_n):
                    act.wait_ge(sem["pt_done"], n("pt_done"))
                    act.activation(dst[:, h, 0:w], seen("act", "pt_done")[:, 0:w], ACT.Copy)\
                       .then_inc(sem["act_released"], 1)

            def ffn1(key):
                norm()

                def one(j):
                    act.wait_ge(sem["up_done"], n("up_done"))
                    act.activation(e4[:, j, :], seen("act", "up_done")[:, 0:S], ACT.Sigmoid)\
                       .then_inc(sem["gate_sigmoid"], 1)
                    n("up_done")
                    seen("act", "up_done")
                with n.loop(act, key + "up", 22 // RING):
                    for j in range(RING):
                        one(j)
                for j in range(22 % RING):
                    one(j)
                if key == "f1":
                    act.wait_ge(sem["sin_in"], n("sin_in"))
                    act.activation(rope[:, :, :, :].rearrange("p a b c -> p (a b c)"),
                                   arena[:, 0:4 * S], ACT.Sin).then_inc(sem["sin_out"], 1)

            def ffn2(key):
                norm()

                def one(j, w=P):
                    act.wait_ge(sem["gate_ready"], n("gate_ready"))
                    act.activation(e4[0:w, j, :], a4[0:w, j, :], ACT.Sigmoid).then_inc(sem["gate_sigmoid"], 1)
                with n.loop(act, key + "up", 22 // RING):
                    for j in range(RING):
                        one(j)
                for j in range(22 % RING):
                    one(j, P if j == 0 else D_FF2 - 21 * P)

            load(posi[:, :], io["positions"][0].partition_broadcast(P), "positions_in")
            act.wait_ge(sem["pool_ready"], 1)
            with n.loop(act, "block1", DEPTH) as l:
                for i, name in enumerate(("ffn1_norm", "mix_norm", "ca_norm", "mem_norm", "ffn2_norm")):
                    load(rows[C * i:C * (i + 1), 0, :], io[name][l].rearrange("(c p) -> c p", p=P), "rows_in")
                load(bcast[:, 0:N_FOX], io["b_fgate"][l].partition_broadcast(P), "bcast_in")
                ffn1("f1")
                norm()
                softplus(lS[:, :, :], zS[:, :, :])
                softplus(lf3[:, :, :], lf3[:, :, :])
                gate_tiles(0, 6)
                exps(zS[:, :, :])
                gate_tiles(6, 6)
                for t in range(T):
                    exps(sc[:, t, 0:N_FOX, 0:P * (t + 1)])
                gate_tiles(12, 6)
                turned(pT, N_FOX, TRI)
                gate_tiles(18, 2)
                for t in range(T):
                    exps(sc[:, t, 0:N_DSA, 0:P * (t + 1)])
                gate_tiles(20, 4)
                turned(pT, N_DSA, TRI)
                act.wait_ge(sem["x_ready"], n("x_ready", 2 * T))
                act.wait_ge(sem["mem_in"], 16)
                square_sums(mem)
                act.wait_ge(sem["hs_free"], n("hs_free"))
                square_sums(x)
                for t in range(T):
                    exps(csc[:, t, :, :])
                turned(cpT, CA_H, T * S)
                ffn1("f2")
            norm()
            load(hT[:, 0:4, :].rearrange("p a b -> p (a b)"), io["final_norm"].partition_broadcast(P), "final_in")
            with n.loop(act, "block2", DEPTH) as l:
                a = 0
                for name, k in (("attn_norm_w_2", 8), ("ffn_norm_w_2", 8), ("ssd_conv_w_2", 32), ("ssd_conv_b_2", 8),
                                ("ssd_norm_w_2", 4), ("sc_conv_w_2", 6)):
                    v = io[name][l]
                    v = v.rearrange("k (c p) -> (k c) p", p=P) if len(v.shape) == 2 else v.rearrange("(c p) -> c p", p=P)
                    load(rows[a:a + k, 0, :], v, "rows_in")
                    a += k
                for tap in range(4):
                    v = io["ffn_conv_w_2"][l, tap, :] if tap < 3 else io["ffn_conv_b_2"][l, :]
                    for half in range(2):
                        r0 = (tap % 2) * 44 + half * 22
                        load(rows[r0:r0 + 21, 1 + tap // 2, :],
                             v[half * D_FF2:half * D_FF2 + 21 * P].rearrange("(c p) -> c p", p=P), "rows_in")
                        load(rows[r0 + 21:r0 + 22, 1 + tap // 2, 0:HD],
                             v[half * D_FF2 + 21 * P:(half + 1) * D_FF2].rearrange("(c p) -> c p", p=HD), "rows_in")
                load(rows[0:CMP_BLOCK, 3, 0:HD], io["cmp_k_pos_2"][l], "rows_in")
                load(rows[0:CMP_BLOCK, 3, HD:P], io["cmp_v_pos_2"][l], "rows_in")
                load(w2s[:, 0:HD], io["cmp_k_w2_2"][l], "bcast_in")
                load(w2s[:, HD:P], io["cmp_k_w2_2"][l], "bcast_in")
                load(w2s[:, P:P + HD], io["cmp_v_w2_2"][l], "bcast_in")
                load(bcast[:, 0:8], io["ssd_dt_bias_2"][l].partition_broadcast(P), "bcast_in")
                load(bcast[:, 8:16], io["ssd_a_log_2"][l].partition_broadcast(P), "bcast_in")
                dv = io["ssd_d_2"][l].rearrange("(i two) -> two i", two=2)
                for k in range(2):
                    load(bcast[HD * k:HD * (k + 1), 16:20], dv[k].partition_broadcast(HD), "bcast_in")
                norm()
                sigmoids((mT0[:, :], 1.0), (zE[:, :, :], 1.0), (g12[:, :, :], 1.0))
                softplus(lf3[:, :, :], lf3[:, :, :])
                exps(anegs[:, :])
                sigmoids((hidE[:, :, :], 2.0 * float(np.sqrt(2.0 / np.pi))))
                exps(mT[:, :, :])
                exps(cmpS[:, :, :, 0:N_CMP])
                for t in range(T):
                    exps(nsc[:, t, :, 0:P * (t + 1)])
                for t in range(T):
                    act.wait_ge(sem["pt_done"], n("pt_done"))
                    act.activation(pcT[0:N_CMP, :, t * P:(t + 1) * P],
                                   seen("act", "pt_done")[0:N_CMP, :].rearrange("p (h q) -> p h q", q=P), ACT.Copy)\
                       .then_inc(sem["act_released"], 1)
                turned(npT, 2 * NSA_H, TRI)
                ffn2("f3")
            norm()
            load(hT[:, 0:4, :].rearrange("p a b -> p (a b)"), io["final_norm_w_2"].partition_broadcast(P), "final_in")

        @block.gpsimd
        def _(pool):
            n = Counts("pool", plan, found)

            def power(dst, src, w):
                pool.wait_ge(sem["ms_done"], n("ms_done"))
                pool.tensor_tensor(dst, src, nhalf[:, 0:1].to_broadcast([P, w]), ALU.pow).then_inc(sem["rstd_done"], 1)

            pool.dma_start(mem[:, :, :], io["mem"][0].rearrange("(t p) d -> p t d", p=P)).then_inc(sem["mem_in"], 16)
            pool.memset(nhalf[:, :], -0.5)
            pool.memset(rows[:, :, :], 0.0)
            pool.memset(lf[:, :, :], 0.0)
            pool.memset(lf3[:, :, :], 0.0)
            pool.drain().then_inc(sem["pool_ready"], 1)
            with n.loop(pool, "block1", DEPTH):
                for _ in range(5):
                    power(rstd[:, :], ms[:, :], 2)
            power(rstd[:, :], ms[:, :], 2)
            with n.loop(pool, "block2", DEPTH):
                power(rstd[:, :], ms[:, :], 2)
                power(topw[:, 1, :], topw[:, 0, :], S)
                power(rstd[:, :], ms[:, :], 2)
            power(rstd[:, :], ms[:, :], 2)

        @block.vector
        def _(v):
            n = Counts("dve", plan, found)
            n("down_used", RING)

            def ts(out_, in_, s1, s2, op0, op1=None):
                if op1 is None:
                    return v.tensor_scalar(out_, in_, s1, None, op0=op0)
                return v.tensor_scalar(out_, in_, s1, s2, op0=op0, op1=op1)

            def tt(out_, a, b, op):
                return v.tensor_tensor(out_, a, b, op)

            def stt(out_, in0, s, in1, op0, op1):
                return v.scalar_tensor_tensor(out_, in0, s, in1, op0=op0, op1=op1)

            def flat(a):
                return a.rearrange("p a b -> p (a b)")

            def rstd_of():
                v.wait_ge(sem["sq_done"], n("sq_done", T))
                ts(ms[:, :], ss[:, :], 1.0 / D, EPS, ALU.mult, ALU.add).then_inc(sem["ms_done"], 1)
                v.wait_ge(sem["rstd_done"], n("rstd_done"))

            def norm(src, g0):
                rstd_of()
                for t in range(T):
                    ts(hs[:, t, :], src[:, t, :], rstd[:, t:t + 1], None, ALU.mult).then_inc(sem["h_scaled"], 1)
                for g in range(C // 2):
                    v.wait_ge(sem["attn_done"], n("attn_done"))
                    tt(hT[:, 2 * g:2 * g + 2, :], seen("dve", "attn_done")[:, :].rearrange("p (c t) -> p c t", t=S),
                       vecs[:, g0 + 2 * g:g0 + 2 * g + 2].unsqueeze(2).to_broadcast([P, 2, S]), ALU.mult)\
                        .then_inc(sem["dve_released"], 1)

            def add_to_x(slots_used, scale):
                v.wait_ge(sem["down_used"], n("down_used", slots_used))
                for t in range(T):
                    for half in range(2):
                        xs = x[:, t, half * 512:(half + 1) * 512]
                        stt(xs, bank[4 + 2 * t + half][:, :], scale, xs, ALU.mult, ALU.add).then_inc(sem["x_ready"], 1)

            def rope_tables():
                ang = arena[:, 0:4 * S].rearrange("p (b f s) -> p b f s", b=2, f=2)
                trn = arena[:, 4 * S:8 * S].rearrange("p (b f s) -> p b f s", b=2, f=2)
                posf = arena[:, 8 * S:9 * S]
                v.wait_ge(sem["positions_in"], 16)
                v.tensor_copy(posf, posi[:, :])
                v.drain()
                for f in range(2):
                    ts(ang[:, 0, f, :], posf, K("inv1"), None, ALU.mult)
                    ts(ang[:, 1, f, :], K("pos2"), K("inv2"), None, ALU.mult)
                v.drain()
                MAGIC = 1.5 * 2.0 ** 23
                TWO_PI = 2.0 * np.pi
                C1 = 6.28125
                C2 = float(np.float32(np.round((TWO_PI - C1) * 2 ** 22) / 2 ** 22))
                C3 = float(np.float32(TWO_PI - C1 - C2))
                for b in range(2):
                    for f, quarter in ((0, 0.25), (1, 0.0)):
                        a_, t_ = ang[:, b, f, :], trn[:, b, f, :]
                        ts(t_, a_, 1.0 / TWO_PI, quarter, ALU.mult, ALU.add)
                        v.drain()
                        ts(t_, t_, MAGIC, None, ALU.add)
                        v.drain()
                        ts(t_, t_, MAGIC, None, ALU.subtract)
                        v.drain()
                        for c_ in (C1, C2, C3):
                            stt(a_, t_, -c_, a_, ALU.mult, ALU.add)
                            v.drain()
                        if f == 0:
                            ts(a_, a_, float(np.pi / 2), None, ALU.add)
                            v.drain()
                        ts(a_, a_, 3.1415925, -3.1415925, ALU.min, ALU.max)
                        v.drain()
                v.drain().then_inc(sem["sin_in"], 1)
                v.wait_ge(sem["sin_out"], n("sin_out"))

            def ffn1(key, g0):
                norm(x, g0)

                def one(f, j):
                    v.wait_ge(sem["gate_sigmoid"], n("gate_sigmoid"))
                    v.wait_ge(sem["up_done"], n("up_done", 2))
                    tt(a4[:, j, :], e4[:, j, :], seen("dve", "up_done")[:, 0:S], ALU.mult)\
                        .then_inc(sem["dve_released"], 1)
                    v.drain()
                    tt(guT[:, f, :], a4[:, j, :], seen("dve", "up_done")[:, 0:S], ALU.mult)\
                        .then_inc(sem["dve_released"], 1)
                with n.loop(v, key + "up", 22 // RING) as i:
                    for j in range(RING):
                        one(i * RING + j, j)
                for j in range(22 % RING):
                    one(22 // RING * RING + j, j)
                if key == "f1":
                    v.drain()
                    rope_tables()
                add_to_x(11, 0.5)

            def col(c, k=1):
                return vecs[:, c:c + k] if isinstance(c, int) else vecs[:, bass.ds(c, k)]

            def conv_ffn(dst, b, w, f, half):
                def vec(tap):
                    c = col(f + (66 + 44 * tap + 22 * half))
                    return c[0:w, :] if w < P else c
                ts(dst, b[0:w, 0:S], vec(2), vec(3), ALU.mult, ALU.add)
                v.drain()
                stt(dst[:, 1:S], b[0:w, 0:S - 1], vec(1), dst[:, 1:S], ALU.mult, ALU.add)
                v.drain()
                return stt(dst[:, 2:S], b[0:w, 0:S - 2], vec(0), dst[:, 2:S], ALU.mult, ALU.add)

            def ffn2(key):
                norm(x, 8)

                def one(f, j, w=P):
                    v.wait_ge(sem["up_done"], n("up_done"))
                    conv_ffn(a4[0:w, j, :], seen("dve", "up_done"), w, f, 0).then_inc(sem["dve_released"], 1)
                    v.drain().then_inc(sem["gate_ready"], 1)
                    v.wait_ge(sem["up_done"], n("up_done"))
                    conv_ffn(b4[0:w, j, :], seen("dve", "up_done"), w, f, 1).then_inc(sem["dve_released"], 1)
                    v.drain()
                    v.wait_ge(sem["gate_sigmoid"], n("gate_sigmoid"))
                    tt(a4[0:w, j, :], a4[0:w, j, :], e4[0:w, j, :], ALU.mult)
                    v.drain()
                    tt(guT[0:w, f, :], a4[0:w, j, :], b4[0:w, j, :], ALU.mult)
                with n.loop(v, key + "up", 22 // RING) as i:
                    for j in range(RING):
                        one(i * RING + j, j)
                for j in range(22 % RING):
                    one(22 // RING * RING + j, j, P if j == 0 else D_FF2 - 21 * P)
                v.drain().then_inc(sem["operand_ready"], 1)
                add_to_x(11, 1.0)

            def vectors(bc_loads, sizes):
                v.wait_ge(sem["bcast_in"], n("bcast_in", bc_loads))
                v.wait_ge(sem["attn_done"], n("attn_done"))
                b, a = seen("dve", "attn_done"), 0
                for g, k in enumerate(sizes):
                    ins = v.tensor_copy(vecs[:, a:a + k], b[:, g * P:g * P + k])
                    a += k
                ins.then_inc(sem["dve_released"], 1)
                v.drain()

            def proj(tiles_all, roped, place, blk, xr_):
                late, tile = [], 0

                def combine(dst, buf, w):
                    v.wait_ge(sem["attn_done"], n("attn_done"))
                    tt(a4[0:w, 0, :], xr_[0:w, buf, :], rope[0:w, blk, 0, :], ALU.mult)
                    tt(a4[0:w, 1, :], seen("dve", "attn_done")[0:w, 0:S], rope[0:w, blk, 1, :], ALU.mult)
                    v.drain()
                    tt(dst, a4[0:w, 0, :], a4[0:w, 1, :], ALU.add).then_inc(sem["dve_released"], 1)
                    v.drain()

                for name, i, _, width in tiles_all:
                    w = P if width < 0 else width
                    if name == "sc" and i >= 4:
                        v.drain()
                    v.wait_ge(sem["proj_done"], n("proj_done"))
                    b = seen("dve", "proj_done")
                    if name in roped:
                        if name == "kv":
                            v.tensor_copy(kvT[HD:P, 0, :], b[HD:P, 0:S])
                        v.tensor_copy(xr_[0:w, tile % 2, :], b[0:w, 0:S]).then_inc(sem["dve_released"], 1)
                    else:
                        place(name, i, w, b)
                    while late:
                        combine(*late.pop(0))
                    if name in roped:
                        if name == "kv":
                            w = HD
                        late.append((roped[name][0:w, i, :], tile % 2, w))
                        tile += 1
                while late:
                    combine(*late.pop(0))

            def softmax_a(p, m, h_n, w):
                v.tensor_reduce(m, p, axis=AX.X, op=ALU.max)
                v.drain()
                tt(p, p, m.unsqueeze(2).to_broadcast([P, h_n, w]), ALU.subtract).then_inc(sem["exp_in"], 1)

            def softmax_b(p, m, h_n, w):
                v.tensor_reduce(m, p, axis=AX.X, op=ALU.add)
                v.drain()
                v.reciprocal(m, m)
                v.drain()
                return tt(p, p, m.unsqueeze(2).to_broadcast([P, h_n, w]), ALU.mult)

            def outputs(dst, count, last_rows=(0, P)):
                for i in range(count):
                    v.wait_ge(sem["attn_done"], n("attn_done"))
                    b = seen("dve", "attn_done")
                    p0, p1 = last_rows if i == count - 1 else (0, P)
                    d = dst(i)
                    v.tensor_copy(d[p0:p1, :], b[p0:p1, 0:S]).then_inc(sem["dve_released"], 1)

            v.wait_ge(sem["io_in"], 32)
            v.wait_ge(sem["pool_ready"], 1)
            v.drain().then_inc(sem["x_ready"], 2 * T)

            with n.loop(v, "block1", DEPTH):
                vectors(16, (5 * C,))
                ffn1("f1", 0)
                norm(x, 8)

                def place1(name, i, w, b):
                    dst = DEST1[name][0:w, i, :]
                    scale = HD ** -0.5 if name in ("fq", "sq") else 1.0
                    ts(dst, b[0:w, 0:S], scale, None, ALU.mult).then_inc(sem["dve_released"], 1)
                proj(UP1, {k: DEST1[k] for k in ROPED}, place1, 0, xr)
                for cols in TOK1:
                    for t in range(T):
                        v.wait_ge(sem["proj_done"], n("proj_done"))
                        b = seen("dve", "proj_done")
                        a = 0
                        for _, w, c in cols:
                            ins = v.tensor_copy(vtok[:, t, c:c + w], b[:, a:a + w])
                            a += w
                        ins.then_inc(sem["dve_released"], 1)
                v.drain()
                for h in range(N_SB):
                    v.wait_ge(sem["attn_done"], n("attn_done"))
                    v.tensor_copy(zS[:, h, :], seen("dve", "attn_done")[:, 0:TRI]).then_inc(sem["dve_released"], 1)
                v.drain().then_inc(sem["softplus_in"], 1)
                z_, l_, lb_, L_ = flat(zS), flat(lS), flat(lbS), flat(LS)
                for t in range(T):
                    tt(lf2[:, t, 0:N_FOX], vtok[:, t, V_FF:V_FF + N_FOX], bcast[:, 0:N_FOX], ALU.add)
                v.drain()
                v.tensor_copy(lf3[:, :, 0:N_FOX], lf2[:, :, 0:N_FOX]).then_inc(sem["softplus_in"], 1)
                v.drain()
                ts(lf2[:, :, 0:N_FOX], lf2[:, :, 0:N_FOX], 0.0, None, ALU.min)
                v.wait_ge(sem["softplus_out"], n("softplus_out"))
                stt(lb_, z_, 0.0, l_, ALU.min, ALU.subtract)
                v.drain()
                tt(L_, lb_, z_, ALU.subtract)
                v.drain()
                strict = K("strict_t").unsqueeze(1).to_broadcast([P, N_SB, TRI])
                tt(LS[:, :, :], LS[:, :, :], strict, ALU.mult).then_inc(sem["operand_ready"], 1)
                v.wait_ge(sem["softplus_out"], n("softplus_out"))
                tt(lf[:, :, 0:N_FOX], lf2[:, :, 0:N_FOX], lf3[:, :, 0:N_FOX], ALU.subtract)
                v.drain()
                ts(lfn[:, :, 0:N_FOX], lf[:, :, 0:N_FOX], -1.0, None, ALU.mult).then_inc(sem["operand_ready"], 1)
                for h in range(N_SB):
                    v.wait_ge(sem["attn_done"], n("attn_done"))
                    tt(zS[:, h, :], seen("dve", "attn_done")[:, 0:TRI], lbS[:, h, :], ALU.add)\
                        .then_inc(sem["dve_released"], 1)
                v.drain().then_inc(sem["exp_in"], 1)
                v.wait_ge(sem["attn_done"], n("attn_done"))
                v.tensor_copy(cq[:, :, :], seen("dve", "attn_done")[:, 0:16].rearrange("p (t h) -> p t h", h=8))\
                 .then_inc(sem["dve_released"], 1)
                v.wait_ge(sem["exp_out"], n("exp_out"))
                tt(zS[:, :, :], zS[:, :, :], strict, ALU.mult).then_inc(sem["operand_ready"], 1)
                outputs(lambda i: oT[:, (5, 6, 7)[i], :], 3, (HD, P))
                for t in range(T):
                    w = P * (t + 1)
                    for g in sharing(N_FOX):
                        v.wait_ge(sem["attn_done"], n("attn_done"))
                        b = seen("dve", "attn_done")
                        for j, h in enumerate(g):
                            ins = stt(sc[:, t, h, 0:w], b[:, j * S:j * S + w], cq[:, t, h:h + 1],
                                      K("causal", P * (1 - t), 2 * P), ALU.add, ALU.add)
                        ins.then_inc(sem["dve_released"], 1)
                ts(lf3[:, :, 0:N_IDX], vtok[:, :, V_IW:V_IW + N_IDX], N_IDX ** -0.5 * HD ** -0.5, None, ALU.mult)
                v.drain()
                for t in range(T):
                    w = P * (t + 1)
                    for g in sharing(N_IDX):
                        v.wait_ge(sem["attn_done"], n("attn_done"))
                        b = seen("dve", "attn_done")[:, :].rearrange("p (h k) -> p h k", h=2)
                        stt(ixs[:, of(g), 0:w], b[:, :, 0:w], 0.0,
                            lf3[:, t, of(g)].unsqueeze(2).to_broadcast([P, 2, w]), ALU.max, ALU.mult)\
                            .then_inc(sem["dve_released"], 1)
                    v.drain()
                    v.tensor_reduce(topw[:, t, 0:w], ixs[:, :, 0:w].rearrange("p h k -> p k h"), axis=AX.X, op=ALU.add)
                    v.drain()
                    tt(topw[:, t, 0:w], topw[:, t, 0:w], K("causal", P * (1 - t), 2 * P), ALU.add)
                    v.drain()
                for t in range(T):
                    w = P * (t + 1)
                    softmax_a(sc[:, t, :, 0:w], smax[:, 0:N_FOX], N_FOX, w)
                    v.drain()
                for t in range(T):
                    w = P * (t + 1)
                    v.wait_ge(sem["exp_out"], n("exp_out"))
                    softmax_b(sc[:, t, :, 0:w], ssum[:, 0:N_FOX], N_FOX, w)
                    v.drain()
                v.drain().then_inc(sem["operand_ready"], 1)
                for t in range(T):
                    s_ = topw[:, t, 0:P * (t + 1)]
                    for _ in range(TOPK // 8):
                        v.max(mx8[:, :], s_)
                        v.drain()
                        v.match_replace(s_, mx8[:, :], s_, TAKEN)
                        v.drain()
                    ts(s_, s_, TAKEN / 2, 1e30, ALU.is_le, ALU.mult)
                    v.drain()
                    stt(dmask[:, t, 0:P * (t + 1)], s_, NEG, K("causal", P * (1 - t), 2 * P), ALU.add, ALU.add)
                v.drain()
                outputs(lambda i: oT[:, i, :], 3)
                for t in range(T):
                    w = P * (t + 1)
                    for g in sharing(N_DSA):
                        v.wait_ge(sem["attn_done"], n("attn_done"))
                        b = seen("dve", "attn_done")[:, :].rearrange("p (h k) -> p h k", h=2)
                        k = len(g)
                        stt(sc[:, t, of(g), 0:w], b[:, 0:k, 0:w], HD ** -0.5,
                            dmask[:, t, 0:w].unsqueeze(1).to_broadcast([P, k, w]), ALU.mult, ALU.add)\
                            .then_inc(sem["dve_released"], 1)
                v.drain()
                for t in range(T):
                    w = P * (t + 1)
                    softmax_a(sc[:, t, 0:N_DSA, 0:w], smax[:, 0:N_DSA], N_DSA, w)
                    v.drain()
                for t in range(T):
                    w = P * (t + 1)
                    v.wait_ge(sem["exp_out"], n("exp_out"))
                    softmax_b(sc[:, t, 0:N_DSA, 0:w], ssum[:, 0:N_DSA], N_DSA, w)
                    v.drain()
                v.drain().then_inc(sem["operand_ready"], 1)
                v.wait_ge(sem["act_released"], n("act_released", 24 + N_FOX))
                n("act_released", N_DSA)
                outputs(lambda i: oT[:, (3, 4, 7)[i], :], 3, (0, HD))
                for m in range(C):
                    for k in range(3):
                        v.wait_ge(sem["proj_done"], n("proj_done"))
                        tt(a4[:, k, :], gates[:, C * k + m, :], seen("dve", "proj_done")[:, 0:S], ALU.mult)\
                            .then_inc(sem["dve_released"], 1)
                    v.drain()
                    tt(a4[:, 0, :], a4[:, 0, :], a4[:, 1, :], ALU.add)
                    v.drain()
                    tt(hsT[:, m, :], a4[:, 0, :], a4[:, 2, :], ALU.add)
                    v.drain()
                v.drain().then_inc(sem["operand_ready"], 1)
                add_to_x(4, 1.0)
                norm(mem, 24)
                v.drain().then_inc(sem["hs_free"], 1)
                for h in range(CA_H):
                    v.wait_ge(sem["proj_done"], n("proj_done"))
                    v.tensor_copy(ckT[:, h, :], seen("dve", "proj_done")[:, 0:S]).then_inc(sem["dve_released"], 1)
                for j in range(2):
                    for t in range(T):
                        v.wait_ge(sem["proj_done"], n("proj_done"))
                        v.tensor_copy(cv[:, t, 2 * P * j:2 * P * (j + 1)], seen("dve", "proj_done")[:, 0:2 * P])\
                         .then_inc(sem["dve_released"], 1)
                norm(x, 16)
                for h in range(CA_H):
                    v.wait_ge(sem["proj_done"], n("proj_done"))
                    v.tensor_copy(cqT[:, h, :], seen("dve", "proj_done")[:, 0:S]).then_inc(sem["dve_released"], 1)
                for t in range(T):
                    for i in range(2):
                        v.wait_ge(sem["attn_done"], n("attn_done"))
                        ts(csc[:, t, 2 * i:2 * i + 2, :], seen("dve", "attn_done")[:, :].rearrange("p (h k) -> p h k", h=2),
                           P ** -0.5, None, ALU.mult).then_inc(sem["dve_released"], 1)
                v.drain()
                for t in range(T):
                    softmax_a(csc[:, t, :, :], smax[:, 0:CA_H], CA_H, S)
                    v.drain()
                for t in range(T):
                    v.wait_ge(sem["exp_out"], n("exp_out"))
                    softmax_b(csc[:, t, :, :], ssum[:, 0:CA_H], CA_H, S)
                    v.drain()
                v.drain().then_inc(sem["operand_ready"], 1)
                outputs(lambda i: coT[:, i, :], CA_H)
                n("act_released", CA_H)
                add_to_x(2, 1.0)
                ffn1("f2", 32)
                pad = pads[0]
                if pad:
                    v.wait_ge(sem["attn_done"], n("attn_done", pad))
                    for _ in range(pad):
                        seen("dve", "attn_done")
                    v.memset(ssum[:, 0:1], 0.0).then_inc(sem["dve_released"], pad)

            gain = hT[:, 0:4, :].rearrange("p a b -> p (a b)")
            rstd_of()
            v.wait_ge(sem["final_in"], 16)
            for t in range(T):
                stt(x[:, t, :], x[:, t, :], rstd[:, t:t + 1], gain, ALU.mult, ALU.mult).then_inc(sem["x_ready"], 2)

            with n.loop(v, "block2", DEPTH):
                vectors(16 * BC2_DMAS, (66, 88, 88, CMP_BLOCK))
                norm(x, 0)

                def place2(name, i, w, b):
                    if name == "z":
                        v.tensor_copy(zT[:, i, :], b[:, 0:S])
                        v.tensor_copy(zE[:, i, :], b[:, 0:S]).then_inc(sem["dve_released"], 1)
                    elif name == "xbc":
                        d = xbc[:, i, :]
                        ts(d, b[:, 0:S], vecs[:, 40 + i:41 + i], vecs[:, 48 + i:49 + i], ALU.mult, ALU.add)
                        for back in (1, 2, 3):
                            v.drain()
                            ins = stt(d[:, back:S], b[:, 0:S - back], vecs[:, 40 + i - 8 * back:41 + i - 8 * back],
                                      d[:, back:S], ALU.mult, ALU.add)
                        ins.then_inc(sem["dve_released"], 1)
                    elif i < 4:
                        v.tensor_copy(scm[:, i, :], b[:, 0:S]).then_inc(sem["dve_released"], 1)
                    else:
                        tt(scm[:, i, :], b[:, 0:S], scm[:, i - 2, :], ALU.mult).then_inc(sem["dve_released"], 1)
                proj(UP2, dict(nq=nqT, kv=kvT, ks=ksT, kw=kwT), place2, 1, xr2)
                for t in range(T):
                    v.wait_ge(sem["proj_done"], n("proj_done"))
                    v.tensor_copy(vtok2[:, t, :], seen("dve", "proj_done")[:, 0:148]).then_inc(sem["dve_released"], 1)
                v.drain()
                pos = vecs[:, 242:242 + CMP_BLOCK]
                for half in range(2):
                    tt(cmpX[:, 16 * half:16 * (half + 1), :],
                       kvT[:, 0, 16 * half:16 * (half + N_CMP)].rearrange("p (n j) -> p j n", j=16),
                       pos[:, 16 * half:16 * (half + 1)].unsqueeze(2).to_broadcast([P, 16, N_CMP]), ALU.add)
                v.drain().then_inc(sem["operand_ready"], 1)
                v.tensor_copy(mT0[:, :], flat(xbc))
                v.tensor_copy(g12[:, :, :], vtok2[:, :, 8 + 2 * HD:148])
                v.drain().then_inc(sem["sigmoid_in"], 1)
                for t in range(T):
                    tt(lf2[:, t, :], vtok2[:, t, 0:8], bcast[:, 0:8], ALU.add)
                v.tensor_copy(anegs[:, :], bcast[:, 8:16])
                v.drain()
                v.tensor_copy(lf3[:, :, :], lf2[:, :, :]).then_inc(sem["softplus_in"], 1)
                v.drain().then_inc(sem["exp_in"], 1)
                for i in range(2):
                    d = yT[:, 4 + i, :]
                    ts(d, scm[:, 4 + i, :], vecs[:, 64 + i:65 + i], None, ALU.mult)
                    for back in (1, 2):
                        v.drain()
                        c_ = 64 + i - 2 * back
                        stt(d[:, back:S], scm[:, 4 + i, 0:S - back], vecs[:, c_:c_ + 1], d[:, back:S], ALU.mult, ALU.add)
                    v.drain()
                    tt(d, d, scm[:, i, :], ALU.mult)
                v.wait_ge(sem["softplus_out"], n("softplus_out"))
                stt(lfn[:, :, :], lf2[:, :, :], 0.0, lf3[:, :, :], ALU.max, ALU.add)
                v.drain()
                v.wait_ge(sem["exp_out"], n("exp_out"))
                for t in range(T):
                    stt(lf[:, t, :], lfn[:, t, :], -1.0, anegs[:, :], ALU.mult, ALU.mult)
                v.wait_ge(sem["sigmoid_out"], n("sigmoid_out"))
                tt(flat(xbc), flat(xbc), mT0[:, :], ALU.mult)
                v.drain().then_inc(sem["operand_ready"], 1)
                tt(flat(zT), flat(zT), flat(zE), ALU.mult)
                v.wait_ge(sem["cmp_done"], n("cmp_done", 2))
                for i in range(2):
                    v.tensor_copy(hid[:, i, 0:N_CMP], seen("dve", "cmp_tile")[:, 0:N_CMP]).then_inc(sem["dve_released"], 1)
                v.drain()
                h_, e_ = hid[:, :, 0:N_CMP], hidE[:, :, :]
                tt(e_, h_, h_, ALU.mult)
                v.drain()
                ts(e_, e_, 0.044715, 1.0, ALU.mult, ALU.add)
                v.drain()
                tt(e_, e_, h_, ALU.mult).then_inc(sem["sigmoid_in"], 1)
                v.wait_ge(sem["sigmoid_out"], n("sigmoid_out"))
                tt(h_, h_, e_, ALU.mult).then_inc(sem["operand_ready"], 1)
                for t in range(T):
                    v.wait_ge(sem["attn_done"], n("attn_done"))
                    tt(xdt[:, t, :].rearrange("p (h d) -> p h d", d=HD),
                       seen("dve", "attn_done")[:, :].rearrange("p (h d) -> p h d", d=HD),
                       lfn[:, t, :].unsqueeze(2).to_broadcast([P, SSD_H, HD]), ALU.mult).then_inc(sem["dve_released"], 1)
                for g in range(2):
                    v.wait_ge(sem["attn_done"], n("attn_done"))
                    v.tensor_copy(cbT[:, g, :], seen("dve", "attn_done")[:, 0:TRI]).then_inc(sem["dve_released"], 1)
                v.wait_ge(sem["attn_done"], n("attn_done"))
                v.tensor_copy(cq[:, :, :], seen("dve", "attn_done")[:, 0:16].rearrange("p (t h) -> p t h", h=8))\
                 .then_inc(sem["dve_released"], 1)
                v.drain()
                for h in range(SSD_H):
                    v.wait_ge(sem["attn_done"], n("attn_done"))
                    b = seen("dve", "attn_done")
                    stt(mT[:, h, 0:S], b[:, 0:S], cq[:, 0, h:h + 1], K("causal_t", 0, S), ALU.subtract, ALU.add)
                    stt(mT[:, h, S:TRI], b[:, P:S], cq[:, 1, h:h + 1], K("causal_t", S, TRI), ALU.subtract, ALU.add)\
                        .then_inc(sem["dve_released"], 1)
                v.drain().then_inc(sem["exp_in"], 1)
                v.wait_ge(sem["attn_done"], n("attn_done"))
                b = seen("dve", "attn_done")
                v.tensor_copy(kcT[:, 0:N_CMP], b[:, 0:N_CMP])
                v.tensor_copy(vcs[0:N_CMP, :], b[0:N_CMP, 16:16 + HD]).then_inc(sem["dve_released"], 1)
                for g in sharing(NSA_H):
                    v.wait_ge(sem["attn_done"], n("attn_done"))
                    b = seen("dve", "attn_done")[:, 0:NSA_H * 16].rearrange("p (t h n) -> p t h n", t=T, h=2)
                    for t in range(T):
                        ins = stt(cmpS[:, t, of(g), 0:N_CMP], b[:, t, :, 0:N_CMP], HD ** -0.5,
                                  K("cmpneg", 16 * t, 16 * t + N_CMP).unsqueeze(1).to_broadcast([P, 2, N_CMP]),
                                  ALU.mult, ALU.add)
                    ins.then_inc(sem["dve_released"], 1)
                for t in range(T):
                    w = P * (t + 1)
                    for k in range(2):
                        for g in sharing(NSA_H):
                            v.wait_ge(sem["attn_done"], n("attn_done"))
                            stt(nsc[:, t, NSA_H * k + g[0]:NSA_H * k + g[1] + 1:2, 0:w],
                                seen("dve", "attn_done")[:, :].rearrange("p (h k) -> p h k", h=2)[:, :, 0:w], HD ** -0.5,
                                K("causal", P * (1 - t), 2 * P).unsqueeze(1).to_broadcast([P, 2, w]), ALU.mult, ALU.add)\
                                .then_inc(sem["dve_released"], 1)
                v.wait_ge(sem["exp_out"], n("exp_out"))
                for g in range(2):
                    m_ = mT[:, 4 * g:4 * g + 4, :]
                    tt(m_, m_, cbT[:, g, :].unsqueeze(1).to_broadcast([P, 4, TRI]), ALU.mult)
                v.drain().then_inc(sem["operand_ready"], 1)
                cs3 = cmpS[:, :, :, :].rearrange("p t h n -> p (t h) n")[:, :, 0:N_CMP]
                softmax_a(cs3, smax[:, 0:8], 8, N_CMP)
                v.drain()
                for t in range(T):
                    w = P * (t + 1)
                    softmax_a(nsc[:, t, :, 0:w], smax[:, 0:8], 8, w)
                    v.drain()
                for i in range(4):
                    v.wait_ge(sem["attn_done"], n("attn_done"))
                    stt(yT[:, i, :], xbc[:, i, :], bcast[:, 16 + i:17 + i], seen("dve", "attn_done")[:, 0:S],
                        ALU.mult, ALU.add).then_inc(sem["dve_released"], 1)
                v.drain()
                y4 = flat(yT[:, 0:4, :])
                tt(y4, y4, flat(zT), ALU.mult)
                v.drain()
                tt(flat(zE), y4, y4, ALU.mult).then_inc(sem["operand_ready"], 1)
                v.wait_ge(sem["exp_out"], n("exp_out"))
                for t in range(T):
                    tt(cmpS[:, t, :, 0:N_CMP], cmpS[:, t, :, 0:N_CMP],
                       K("cmp01", 16 * t, 16 * t + N_CMP).unsqueeze(1).to_broadcast([P, NSA_H, N_CMP]), ALU.mult)
                v.drain()
                v.tensor_reduce(ssum[:, 0:8], cs3, axis=AX.X, op=ALU.add)
                v.drain()
                ts(ssum[:, 0:8], ssum[:, 0:8], 1e-20, None, ALU.max)
                v.drain()
                v.reciprocal(ssum[:, 0:8], ssum[:, 0:8])
                v.drain()
                tt(ssum[:, 0:8].rearrange("p (t h) -> p t h", t=T), ssum[:, 0:8].rearrange("p (t h) -> p t h", t=T),
                   g12[:, :, :].rearrange("p t (h b) -> p t h b", b=3)[:, :, :, 0], ALU.mult)
                v.drain()
                tt(cs3, cs3, ssum[:, 0:8].unsqueeze(2).to_broadcast([P, 8, N_CMP]), ALU.mult)
                v.drain()
                v.wait_ge(sem["attn_done"], n("attn_done"))
                ts(topw[:, 0, :], seen("dve", "attn_done")[:, 0:S], 1.0 / SSD_W, EPS, ALU.mult, ALU.add)\
                    .then_inc(sem["dve_released"], 1)
                v.drain().then_inc(sem["ms_done"], 1)
                for t in range(T):
                    w = P * (t + 1)
                    v.wait_ge(sem["exp_out"], n("exp_out"))
                    v.tensor_reduce(ssum[:, 0:8], nsc[:, t, :, 0:w], axis=AX.X, op=ALU.add)
                    v.drain()
                    v.reciprocal(ssum[:, 0:8], ssum[:, 0:8])
                    v.drain()
                    for k in range(2):
                        tt(ssum[:, 4 * k:4 * k + 4], ssum[:, 4 * k:4 * k + 4],
                           g12[:, t, :].rearrange("p (h b) -> p h b", b=3)[:, :, 1 + k], ALU.mult)
                    v.drain()
                    tt(nsc[:, t, :, 0:w], nsc[:, t, :, 0:w], ssum[:, 0:8].unsqueeze(2).to_broadcast([P, 8, w]), ALU.mult)
                    v.drain()
                v.drain().then_inc(sem["operand_ready"], 1)
                v.wait_ge(sem["rstd_done"], n("rstd_done"))
                for i in range(4):
                    stt(yT[:, i, :], yT[:, i, :], vecs[:, 56 + i:57 + i], topw[:, 1, :], ALU.mult, ALU.mult)
                outputs(lambda i: yT[:, 6 + i, :], 2)
                v.drain().then_inc(sem["operand_ready"], 1)
                add_to_x(4, 1.0)
                ffn2("f3")
                pad = pads[1]
                if pad:
                    v.wait_ge(sem["attn_done"], n("attn_done", pad))
                    for _ in range(pad):
                        seen("dve", "attn_done")
                    v.memset(ssum[:, 0:1], 0.0).then_inc(sem["dve_released"], pad)
            rstd_of()
            v.wait_ge(sem["final_in"], 32)
            for t in range(T):
                stt(hs[:, t, :], x[:, t, :], rstd[:, t:t + 1], gain, ALU.mult, ALU.mult).then_inc(sem["out_ready"], 1)




_INS = ["x", "mem", "positions", "ffn1_norm", "ffn1_w_gu", "ffn1_w_down", "mix_norm", "w_in", "b_fgate", "w_fox_out",
        "w_dsa_out", "w_sb_out", "w_out", "ca_norm", "mem_norm", "ca_w_q", "ca_w_kv", "ca_w_o", "ffn2_norm",
        "ffn2_w_gu", "ffn2_w_down", "final_norm", "attn_norm_w_2", "w_in_2", "ssd_conv_w_2", "ssd_conv_b_2",
        "ssd_dt_bias_2", "ssd_a_log_2", "ssd_d_2", "ssd_norm_w_2", "sc_conv_w_2", "cmp_k_pos_2", "cmp_k_w1_2",
        "cmp_k_w2_2", "cmp_v_pos_2", "cmp_v_w1_2", "cmp_v_w2_2", "w_out_2", "ffn_norm_w_2", "ffn_w_up_2",
        "ffn_conv_w_2", "ffn_conv_b_2", "ffn_w_down_2", "final_norm_w_2"]


def kernel(**inputs):
    import numpy as _np
    import concourse.bacc as _bacc
    from concourse import mybir as _mybir
    from concourse.bass_utils import run_bass_kernel_spmd as _run

    arrays = {f"in_{name}": _np.ascontiguousarray(inputs[name]) for name in _INS}
    arrays["in_consts"] = constants()[1]
    plan = {}
    for _ in range(2):
        nc = _bacc.Bacc("TRN2", target_bir_lowering=False, num_devices=1)
        io = {k[3:]: nc.dram_tensor(k, a.shape, _mybir.dt.from_np(a.dtype), kind="ExternalInput").ap()
              for k, a in arrays.items()}
        out = nc.dram_tensor("out_0", (1, S, D), F32, kind="ExternalOutput").ap()
        found = {}
        build(nc, io, out, plan, found)
        plan = found
    r = _run(nc, [arrays], core_ids=[0])
    return r.results[0]["out_0"]
```
